# Optimizing a Trainium2 kernel written in Bass

```python
import math
import jax, jax.numpy as jnp
from jax import lax
import numpy as np

D_MODEL = 1024
BATCH = 1
SEQ = 256
DEPTH = 1

HEAD_DIM = 64
A_Q_HEADS = D_MODEL // HEAD_DIM
A_KV_HEADS = A_Q_HEADS // 4
A_HALF_WINDOW = 128
B_GROUPS = ((128, 1), (512, 4), (2048, 16))
B_HEADS_PER_GROUP = 4
B_N_HEADS = B_HEADS_PER_GROUP * len(B_GROUPS)
TOTAL_BIAS_HEADS = A_Q_HEADS + B_N_HEADS
N_BUCKETS = 32
MAX_DISTANCE = 1024
N_EXPERTS = 32
TOP_K = 4
D_FF = D_MODEL
SWIGLU_LIMIT = 7.0
SWIGLU_ALPHA = 1.702
EPS = 1e-5
NEG_INF = -1e30

A_Q_W = A_Q_HEADS * HEAD_DIM
A_KV_W = A_KV_HEADS * HEAD_DIM
B_QKV_W = B_N_HEADS * HEAD_DIM
B_OUT_W = B_HEADS_PER_GROUP * HEAD_DIM
IN_WIDTHS = (A_Q_W, A_KV_W, A_KV_W, B_QKV_W, B_QKV_W, B_QKV_W, D_MODEL, D_MODEL)
IN_WIDTH = sum(IN_WIDTHS)

kernel_name = "hybrid_gated_window_dilated_attn_moe"

def rmsnorm(x, g):
    xf = x.astype(jnp.float32)
    y = xf * lax.rsqrt(jnp.mean(xf * xf, axis=-1, keepdims=True) + EPS)
    return (y * g.astype(jnp.float32)).astype(x.dtype)

def t5_buckets(rel):
    half = N_BUCKETS // 2
    max_exact = half // 2
    ret = np.where(rel > 0, half, 0)
    n = np.abs(rel)
    large = max_exact + (np.log(np.maximum(n, 1) / max_exact)
                         / np.log(MAX_DISTANCE / max_exact) * (half - max_exact)).astype(np.int32)
    large = np.minimum(large, half - 1)
    return (ret + np.where(n < max_exact, n, large)).astype(np.int32)

def banded_attention(q, k, v, half_window, dilation, bias_table, sink, valid_len):
    n, L, hkv, g, dh = q.shape
    W = half_window
    nb = L // W
    qb = q.reshape(n, nb, W, hkv, g, dh)

    def band(t):
        tp = jnp.pad(t, ((0, 0), (W, W), (0, 0), (0, 0))).reshape(n, nb + 2, W, hkv, dh)
        return jnp.concatenate([tp[:, :-2], tp[:, 1:-1], tp[:, 2:]], axis=2)

    kb, vb = band(k), band(v)
    off = np.arange(3 * W)[None, :] - W - np.arange(W)[:, None]
    kpos = np.arange(nb)[:, None] * W + np.arange(3 * W)[None, :] - W
    mask = (np.abs(off) <= W)[None] & ((kpos >= 0) & (kpos < valid_len))[:, None, :]
    bias = bias_table[t5_buckets(off * dilation)].astype(jnp.float32)
    bias = jnp.transpose(bias, (2, 0, 1)).reshape(hkv, g, 1, W, 3 * W)

    s = jnp.einsum('nbqhgd,nbkhd->nhgbqk', qb, kb).astype(jnp.float32) * (dh ** -0.5) + bias
    s = jnp.where(mask, s, NEG_INF)
    m = jnp.max(s, axis=-1, keepdims=True)
    if sink is not None:
        sk = sink.astype(jnp.float32).reshape(hkv, g, 1, 1, 1)
        m = jnp.maximum(m, sk)
    p = jnp.exp(s - m)
    denom = jnp.sum(p, axis=-1, keepdims=True)
    if sink is not None:
        denom = denom + jnp.exp(sk - m)
    out = jnp.einsum('nhgbqk,nbkhd->nbqhgd', p / denom, vb.astype(jnp.float32)).astype(q.dtype)
    lse = (m + jnp.log(denom))[..., 0]
    return out.reshape(n, L, hkv, g, dh), lse.reshape(n, hkv, g, L)

def windowed_gqa(q, k, v, sinks, rel_bias):
    b, s = q.shape[:2]
    qg = q.reshape(b, s, A_KV_HEADS, A_Q_HEADS // A_KV_HEADS, HEAD_DIM)
    out, _ = banded_attention(qg, k, v, A_HALF_WINDOW, 1, rel_bias[:, :A_Q_HEADS], sinks, s)
    return out.reshape(b, s, A_Q_W)

def dilated_attention(q, k, v, rel_bias):
    b, s = q.shape[:2]
    H = B_HEADS_PER_GROUP
    outs, lses = [], []
    for gi, (window, dil) in enumerate(B_GROUPS):
        hw = window // (2 * dil)
        L = s // dil
        Lp = -(-L // hw) * hw

        def to_sub(t):
            t = t.reshape(b, L, dil, H, HEAD_DIM).transpose(0, 2, 1, 3, 4).reshape(b * dil, L, H, HEAD_DIM)
            return jnp.pad(t, ((0, 0), (0, Lp - L), (0, 0), (0, 0)))

        c0 = A_Q_HEADS + gi * H
        o, l = banded_attention(to_sub(q[:, :, gi])[:, :, :, None], to_sub(k[:, :, gi]), to_sub(v[:, :, gi]),
                                hw, dil, rel_bias[:, c0:c0 + H], None, L)
        o = o[:, :L, :, 0].reshape(b, dil, L, H, HEAD_DIM).transpose(0, 2, 1, 3, 4).reshape(b, s, H, HEAD_DIM)
        l = l[:, :, 0, :L].reshape(b, dil, H, L).transpose(0, 3, 1, 2).reshape(b, s, H)
        outs.append(o)
        lses.append(l)
    w = jax.nn.softmax(jnp.stack(lses, axis=0), axis=0)
    y = jnp.sum(w[..., None] * jnp.stack(outs, axis=0).astype(jnp.float32), axis=0)
    return y.astype(q.dtype).reshape(b, s, B_OUT_W)

def moe(h, router_w, router_b, w_gate, b_gate, w_up, b_up, w_down, b_down):
    b, s, d = h.shape
    hf = h.reshape(b * s, d)
    logits = (hf @ router_w + router_b).astype(jnp.float32)
    top_val, top_idx = lax.top_k(logits, TOP_K)
    probs = jax.nn.softmax(top_val, axis=-1)
    combine = jnp.sum(jax.nn.one_hot(top_idx, N_EXPERTS, dtype=jnp.float32) * probs[..., None], axis=1)
    y = jnp.zeros((b * s, d), jnp.float32)
    for e in range(N_EXPERTS):
        gate = jnp.minimum(hf @ w_gate[e] + b_gate[e], SWIGLU_LIMIT)
        up = jnp.clip(hf @ w_up[e] + b_up[e], -SWIGLU_LIMIT, SWIGLU_LIMIT)
        act = gate * jax.nn.sigmoid(SWIGLU_ALPHA * gate) * (up + 1.0)
        y = y + combine[:, e:e + 1] * (act @ w_down[e] + b_down[e])
    return y.astype(h.dtype).reshape(b, s, d)

def setup_inputs(seed: int = 0) -> dict:
    key = jax.random.key(seed)
    ks = jax.random.split(key, 20)
    nrm = jax.random.normal
    f32 = jnp.float32
    Ly = DEPTH
    return {
        "x": nrm(ks[0], (BATCH, SEQ, D_MODEL), f32),
        "norm_mix": 1.0 + 0.02 * nrm(ks[1], (Ly, D_MODEL), f32),
        "w_in": nrm(ks[2], (Ly, D_MODEL, IN_WIDTH), f32) * D_MODEL ** -0.5,
        "b_in": 0.02 * nrm(ks[3], (Ly, IN_WIDTH), f32),
        "sinks": 0.5 * nrm(ks[4], (Ly, A_Q_HEADS), f32),
        "rel_bias": 0.2 * nrm(ks[5], (N_BUCKETS, TOTAL_BIAS_HEADS), f32),
        "w_branch_a": nrm(ks[6], (Ly, A_Q_W, D_MODEL), f32) * A_Q_W ** -0.5,
        "w_branch_b": nrm(ks[7], (Ly, B_OUT_W, D_MODEL), f32) * B_OUT_W ** -0.5,
        "w_out": nrm(ks[8], (Ly, D_MODEL, D_MODEL), f32) * D_MODEL ** -0.5,
        "norm_ffn": 1.0 + 0.02 * nrm(ks[9], (Ly, D_MODEL), f32),
        "router_w": nrm(ks[10], (Ly, D_MODEL, N_EXPERTS), f32) * D_MODEL ** -0.5,
        "router_b": 0.01 * nrm(ks[11], (Ly, N_EXPERTS), f32),
        "w_gate": nrm(ks[12], (Ly, N_EXPERTS, D_MODEL, D_FF), f32) * D_MODEL ** -0.5,
        "b_gate": 0.01 * nrm(ks[13], (Ly, N_EXPERTS, D_FF), f32),
        "w_up": nrm(ks[14], (Ly, N_EXPERTS, D_MODEL, D_FF), f32) * D_MODEL ** -0.5,
        "b_up": 0.01 * nrm(ks[15], (Ly, N_EXPERTS, D_FF), f32),
        "w_down": nrm(ks[16], (Ly, N_EXPERTS, D_FF, D_MODEL), f32) * D_FF ** -0.5,
        "b_down": 0.01 * nrm(ks[17], (Ly, N_EXPERTS, D_MODEL), f32),
        "norm_final": 1.0 + 0.02 * nrm(ks[18], (D_MODEL,), f32),
    }

def reference(x, norm_mix, w_in, b_in, sinks, rel_bias, w_branch_a, w_branch_b, w_out,
              norm_ffn, router_w, router_b, w_gate, b_gate, w_up, b_up, w_down, b_down, norm_final):
    b, s, _ = x.shape
    split_points = [int(c) for c in np.cumsum(IN_WIDTHS)[:-1]]
    for layer in range(DEPTH):
        h = rmsnorm(x, norm_mix[layer])
        proj = h @ w_in[layer] + b_in[layer]
        qa, ka, va, qb, kb, vb, ga, gb = jnp.split(proj, split_points, axis=-1)
        ya = windowed_gqa(qa.reshape(b, s, A_Q_HEADS, HEAD_DIM),
                          ka.reshape(b, s, A_KV_HEADS, HEAD_DIM),
                          va.reshape(b, s, A_KV_HEADS, HEAD_DIM),
                          sinks[layer], rel_bias)
        grp = (b, s, len(B_GROUPS), B_HEADS_PER_GROUP, HEAD_DIM)
        yb = dilated_attention(qb.reshape(grp), kb.reshape(grp), vb.reshape(grp), rel_bias)
        merged = (jax.nn.sigmoid(ga) * (ya @ w_branch_a[layer])
                  + jax.nn.sigmoid(gb) * (yb @ w_branch_b[layer]))
        x = x + merged @ w_out[layer]
        h2 = rmsnorm(x, norm_ffn[layer])
        x = x + moe(h2, router_w[layer], router_b[layer], w_gate[layer], b_gate[layer],
                    w_up[layer], b_up[layer], w_down[layer], b_down[layer])
    return rmsnorm(x, norm_final)


_drawn_inputs = setup_inputs


def setup_inputs(seed=0):
    import zlib

    import numpy as np

    out = dict(_drawn_inputs(seed))
    spreads = {}
    factors = {'sinks': 64.0,
     'b_gate': 25.131,
     'b_up': 36.86,
     'b_down': 24.117,
     'norm_final': 24.43,
     'norm_mix': 2.826,
     'router_b': 4.802}
    for name, (base, spread) in spreads.items():
        noise = np.random.default_rng([zlib.crc32(name.encode()), seed]).standard_normal(out[name].shape)
        drawn = base * np.exp(spread * noise) if base else spread * noise
        out[name] = __import__('jax').numpy.asarray(drawn.astype(out[name].dtype))
    for name, factor in factors.items():
        out[name] = (out[name] * factor).astype(out[name].dtype)
    return out
```

```python
from contextlib import ExitStack

import numpy as np

import concourse.bass as bass
from concourse import mybir

F32 = mybir.dt.float32
I32 = mybir.dt.int32
ALU = mybir.AluOpType
ACT = mybir.ActivationFunctionType
AX = mybir.AxisListType

P = 128
BANK = 512
S, D = 256, 1024
TT = S // P
KC = D // P
DH = 64
QA, KVA = 16, 4
HB, NG = 4, 3
DILATION = (1, 4, 16)
B_HALF = 64
A_HALF = 128
NU = QA + HB * NG
BUCKETS, MAX_DISTANCE = 32, 1024
E, TOPK = 32, 4
CAP = 64
PASSES = S // CAP
FAR = 1000.0
LIMIT, ALPHA, EPS, NEG = 7.0, 1.702, 1e-5, -1e30
SCALE = DH ** -0.5

T_QA, T_KA, T_VA, T_QB, T_KB, T_VB, T_GA, T_GB, T_END = np.cumsum(
    [0, QA * DH, KVA * DH, KVA * DH, HB * NG * DH, HB * NG * DH, HB * NG * DH, D, D]) // P
W_BLOCK = 512
IN_WIDTH = int(T_END) * P
N_BLOCKS = -(-IN_WIDTH // W_BLOCK)

SLOT = 2 * D
SLOTS = 12
RING = SLOTS * SLOT // (KC * W_BLOCK)
QUADS = KC // 2


def t5_buckets(rel):
    half = BUCKETS // 2
    exact = half // 2
    n = np.abs(rel)
    large = exact + (np.log(np.maximum(n, 1) / exact) / np.log(MAX_DISTANCE / exact) * (half - exact)).astype(np.int32)
    return (np.where(rel > 0, half, 0) + np.where(n < exact, n, np.minimum(large, half - 1))).astype(np.int32)


def constants():
    square = np.zeros((P, 4 * P), np.float32)
    square[:, 0:P] = np.eye(P)
    square[:, P:2 * P] = np.triu(np.ones((P, P)), 1)
    square[:, 2 * P:3 * P] = 1.0
    square[:, 3 * P:4 * P] = np.arange(P) % CAP
    rel = np.arange(2 * S) - (S - 1)
    onehot = (t5_buckets(rel)[None, :] == np.arange(BUCKETS)[:, None]).astype(np.float32)
    mask = np.zeros((NU, 2 * S), np.float32)
    mask[:QA, np.abs(rel) > A_HALF] = NEG
    for g, d in enumerate(DILATION):
        mask[QA + g * HB:QA + (g + 1) * HB, (rel % d != 0) | (np.abs(rel) > B_HALF * d)] = NEG
    return {"square": square, "onehot": onehot, "mask": mask}


def projection_jobs():
    jobs = []
    for b in range(N_BLOCKS):
        lo, hi = b * W_BLOCK, min((b + 1) * W_BLOCK, IN_WIDTH)
        c = lo
        while c < hi:
            t = c // P
            if T_VA <= t < T_QB or T_VB <= t < T_GA:
                end = min(hi, int(T_QB if t < T_QB else T_GA) * P)
                jobs += [(b, "values", c, end - c, tt) for tt in range(TT)]
                c = end
            else:
                jobs.append((b, "turned", c, P, t))
                c += P
    return jobs


def build(nc, io, out, scratch):
    jobs = projection_jobs()
    qkv_jobs = [j for j in jobs if j[2] < T_GA * P]
    gate_jobs = [j for j in jobs if j[2] >= T_GA * P]

    def jobs_through(b):
        return sum(j[0] <= b for j in jobs)

    groups = [("A", [2 * n, 2 * n + 1]) for n in range(QA // 2)]
    groups += [("B", [QA + g * HB + h for g in range(NG)]) for h in range(HB)]
    first_unit = [sum(len(u) for _, u in groups[:n]) for n in range(len(groups) + 1)]
    unit_heads = [h for _, heads in groups for h in heads]
    GA_N = QA // 2

    ctx = ExitStack()
    front = ExitStack()

    def sb(name, shape, dt=F32, where=ctx):
        return where.enter_context(nc.sbuf_tensor(name, shape, dt))

    def sem(name):
        return ctx.enter_context(nc.semaphore(name))

    with ctx:
        psum = ctx.enter_context(nc.psum_tensor("psum", [P, 8 * BANK], F32))

        def bank(i, n=1):
            return psum[:, i * BANK:(i + n) * BANK]

        ring = sb("ring", [P, SLOTS * SLOT])
        square = sb("square_sb", [P, 4, P])
        ident, tri, ones, slots = (square[:, i, :] for i in range(4))
        x_sb = sb("x_sb", [P, TT, D])
        columns = sb("columns", [P, int(T_END) + KC])
        gu_bias = sb("gu_bias", [P, E, KC, 2])
        stats = sb("stats", [P, 32])

        def fb(name, shape):
            return sb(name, shape, F32, front)

        rows = fb("rows", [int(T_END) + KC, P])
        rel_sb = fb("rel_sb", [BUCKETS, NU])
        sinks = fb("sinks_sb", [P, QA])
        hT = fb("hT", [P, KC, S])
        qaT = fb("qaT", [P, QA // 2, S])
        kaT = fb("kaT", [P, KVA, S])
        qbT = fb("qbT", [P, HB * NG // 2, S])
        kbT = fb("kbT", [P, HB * NG // 2, S])
        va = fb("va", [P, TT, KVA * DH])
        vb = fb("vb", [P, TT, HB * NG * DH])
        gates = fb("gates", [P, 2, KC, S])
        BIAS_RING = 4
        windows = fb("windows", [P, BIAS_RING, 3 * P])
        probs = fb("probs", [P, 2, NG, 2, S])
        probsT = fb("probsT", [P, 2, NG, TT, 2, P])
        mix = fb("mix", [P, TT, D + HB * DH])
        peak = fb("peak", [P, 3, 4])
        minus_peak = fb("minus_peak", [P, 3, 4])
        den = fb("den", [P, 3, 4])
        sink_exp = fb("sink_exp", [P, 3, 4])
        h = mix[:, :, 0:D]
        probs_flat = probs[:, :, :, :, :].rearrange("p a b c d -> p (a b c d)")
        bias_rows = probs_flat[0:E, 0:2 * D].rearrange("p (j n) -> p j n", j=2)
        onehot = probs_flat[0:BUCKETS, 2 * D:2 * D + 2 * S]
        table = probs_flat[0:NU, 2 * D + 2 * S:2 * D + 4 * S]
        products = windows[:, :, :].rearrange("p w n -> p (w n)")[:, 0:4 * S].rearrange(
            "p (i j s) -> p i j s", i=2, j=2)
        value_bias = probsT[0:1].rearrange("p a b c d e -> p (a b c d e)")[:, 0:(KVA + HB * NG) * DH]
        mixT = qaT[:, :, :]
        mixTb = kaT[:, 0:HB * DH // P, :]
        mergedT = hT[:, :, :]
        front.close()

        h2 = sb("h2", [P, TT, D])
        h2T = sb("h2T", [P, KC, S])
        gain_ffn = sb("gain_ffn", [P, D])
        gain_final = sb("gain_final", [P, D])
        router = sb("router", [P, KC, E])
        router_row = sb("router_row", [1, E])
        down_bias = sb("down_bias", [E, D])
        logits = sb("logits", [P, TT, E])
        top8 = sb("top8", [P, TT, 8])
        chosen = sb("chosen", [P, TT, E])
        at_edge = sb("at_edge", [P, TT, E])
        running = sb("running", [P, TT, E])
        weight = sb("weight", [P, TT, E])
        few = sb("few", [P, 16])
        weightT = sb("weightT", [E, S])
        rank = sb("rank", [P, TT, PASSES * E + 1])
        passes = sb("passes", [1, 1], I32)
        pick = sb("pick", [P, TT, CAP])
        spread = sb("spread", [P, TT, 2 * CAP])
        spreadT = sb("spreadT", [P, S])
        xT = sb("xT", [P, KC, CAP])
        gu = sb("gu", [P, D])
        guT = sb("guT", [P, KC, 2, CAP])
        gate_c = sb("gate_c", [P, KC, CAP])
        up_c = sb("up_c", [P, KC, CAP])
        sig = sb("sig", [P, KC, CAP])
        hidden = sb("hidden", [P, KC, CAP])
        y_half = sb("y_half", [P, BANK])
        squares = h2T[:, :, :].rearrange("p (t c) s -> p t (c s)", t=TT)

        x_in, square_in, rows_in, table_in, gu_bias_in, sinks_in = (sem(n) for n in (
            "x_in", "square_in", "rows_in", "table_in", "gu_bias_in", "sinks_in"))
        block_in = [sem(f"block_in{i}") for i in range(RING)]
        wa_in, wb_in, wout_in = sem("wa_in"), sem("wb_in"), sem("wout_in")
        sumsq_done, vec, x2_done = sem("sumsq_done"), sem("vec"), sem("x2_done")
        inverse_done, root_done = sem("inverse_done"), sem("root_done")
        h_done, columns_up, columns_done, table_up, table_done = (sem(n) for n in (
            "h_done", "columns_up", "columns_done", "table_up", "table_done"))
        gu_bias_up, gu_bias_done, hT_up, hT_done = (sem(n) for n in ("gu_bias_up", "gu_bias_done", "hT_up", "hT_done"))
        table_out = sem("table_out")
        window_in = [sem(f"window_in{i}") for i in range(BIAS_RING)]
        job_up, qkv_copied, keys_done, gate_copied = (sem(n) for n in (
            "job_up", "qkv_copied", "keys_done", "gate_copied"))
        scores_up, logits_done, peaks_done, sinks_sub, exps_done, sinks_done = (sem(n) for n in (
            "scores_up", "logits_done", "peaks_done", "sinks_sub", "exps_done", "sinks_done"))
        turned_up, turned_copied, pv_up, mix_done = (sem(n) for n in (
            "turned_up", "turned_copied", "pv_up", "mix_done"))
        gates_done, mixT_up, mixT_done, branch_up, products_done, merged_done, out_up = (sem(n) for n in (
            "gates_done", "mixT_up", "mixT_done", "branch_up", "products_done", "merged_done", "out_up"))
        moe_in, h2_done, h2T_up, h2T_done, logits_up, shift_done, exp_done = (sem(n) for n in (
            "moe_in", "h2_done", "h2T_up", "h2T_done", "logits_up", "shift_done", "exp_done"))
        chosen_done, rank_up, passes_done, weight_done, weightT_up, weightT_done, zeroed = (sem(n) for n in (
            "chosen_done", "rank_up", "passes_done", "weight_done", "weightT_up", "weightT_done", "zeroed"))
        gate_in = [sem(f"gate_in{i}") for i in range(QUADS)]
        up_in = [sem(f"up_in{i}") for i in range(QUADS)]
        down_in = [sem(f"down_in{i}") for i in range(QUADS)]
        gu_used, down_used = sem("gu_used"), sem("down_used")
        pick_done, spread_done, gather_up, xT_done, spreadT_up, spreadT_done = (sem(n) for n in (
            "pick_done", "spread_done", "gather_up", "xT_done", "spreadT_up", "spreadT_done"))
        gu_left, gu_right, guT_up, guT_done, gate_done, sig_done, up_done, gated_done, hidden_done, y_copied = (
            sem(n) for n in ("gu_left", "gu_right", "guT_up", "guT_done", "gate_done", "sig_done", "up_done",
                             "gated_done", "hidden_done", "y_copied"))
        y_up, result_done, y_out = sem("y_up"), sem("result_done"), sem("y_out")
        block = ctx.enter_context(nc.Block())

        def ring_block(b):
            at = (b % RING) * 2 * SLOT
            return ring[:, at:at + KC * W_BLOCK].rearrange("p (c n) -> p c n", c=KC)

        def ring_slot(s, n=1):
            return ring[:, s * SLOT:(s + n) * SLOT].rearrange("p (c n) -> p c n", n=D)

        WA, WB, WOUT = 0, 4, 8
        wa, wb, wout = ring_slot(WA, 4), ring_slot(WB, 1), ring_slot(WOUT, 4)
        gate_w = [ring_slot(2 * q) for q in range(QUADS)]
        up_w = [ring_slot(2 * q + 1) for q in range(QUADS)]
        down_w = [ring_slot(8 + q) for q in range(QUADS)]
        PROJ, SCORE, TURN, PV = (0, 1), (2, 3), (4, 5), (6, 7)
        GU, GATHER, DOWN, Y = 0, 2, 3, 4

        def window(u):
            w = windows[:, u % BIAS_RING, :]
            return bass.AP(w.tensor, w.offset, [list(w.ap[0]), [P, 2], [1, S]])

        @block.sync
        def _(sp):
            sp.dma_start(x_sb[:, :, :], io["x"][0].rearrange("(t p) d -> p t d", p=P)).then_inc(x_in, 16)
            w_in = io["w_in"][0].rearrange("(c p) n -> p c n", p=P)
            for b in range(N_BLOCKS):
                if b >= RING:
                    sp.wait_ge(job_up, jobs_through(b - RING))
                lo, hi = b * W_BLOCK, min((b + 1) * W_BLOCK, IN_WIDTH)
                sp.dma_start(ring_block(b)[:, :, 0:hi - lo], w_in[:, :, lo:hi]).then_inc(block_in[b % RING], 16)
            sp.wait_ge(job_up, jobs_through(N_BLOCKS - RING + 1))
            sp.dma_start(wa, io["w_branch_a"][0].rearrange("(c p) n -> p c n", p=P)).then_inc(wa_in, 16)
            sp.wait_ge(job_up, jobs_through(N_BLOCKS - RING + 2))
            sp.dma_start(wb, io["w_branch_b"][0].rearrange("(c p) n -> p c n", p=P)).then_inc(wb_in, 16)
            sp.wait_ge(job_up, len(jobs))
            sp.dma_start(wout, io["w_out"][0].rearrange("(c p) n -> p c n", p=P)).then_inc(wout_in, 16)

            wg = io["w_gate"][0].rearrange("e (q c p) n -> e q p c n", c=2, p=P)
            wu = io["w_up"][0].rearrange("e (q c p) n -> e q p c n", c=2, p=P)
            wd = io["w_down"][0].rearrange("e (q c p) n -> e q p c n", c=2, p=P)

            def load_expert(e, it):
                for q in range(QUADS):
                    sp.wait_ge(gu_used, it * QUADS + q + 1)
                    sp.dma_start(gate_w[q], wg[bass.ds(e, 1), q].rearrange("o p c n -> (o p) c n")).then_inc(gate_in[q], 16)
                    sp.dma_start(up_w[q], wu[bass.ds(e, 1), q].rearrange("o p c n -> (o p) c n")).then_inc(up_in[q], 16)
                for q in range(QUADS):
                    sp.wait_ge(down_used, it * QUADS + q + 1)
                    sp.dma_start(down_w[q], wd[bass.ds(e, 1), q].rearrange("o p c n -> (o p) c n")).then_inc(down_in[q], 16)

            with sp.Fori(0, E) as e:
                load_expert(e, e)
            sp.wait_ge(passes_done, 1)
            n = sp.value_load(passes[0:1, 0:1], min_val=1, max_val=PASSES)
            with sp.If(n > 1):
                with sp.Fori(1, n) as p:
                    with sp.Fori(0, E) as e:
                        load_expert(e, p * E + e)
            for tt in range(TT):
                sp.wait_ge(result_done, tt + 1)
                sp.dma_start(out[0, tt * P:(tt + 1) * P, :], h2[:, tt, :]).then_inc(y_out, 16)
            sp.wait_ge(y_out, 16 * TT)

        @block.gpsimd
        def _(pool):
            pool.wait_ge(table_out, 16)
            for u, head in enumerate(unit_heads):
                if u >= BIAS_RING:
                    pool.wait_ge(logits_done, u - BIAS_RING + 1)
                src = bass.AP(scratch.tensor, head * 2 * S, [[1, P], [1, 3 * P]])
                pool.dma_start(windows[:, u % BIAS_RING, :], src).then_inc(window_in[u % BIAS_RING], 16)

        @block.scalar
        def _(act):
            def root(k):
                r = stats[:, 8 * k:8 * k + TT]
                act.wait_ge(inverse_done, k + 1)
                nc.scalar.activation(r, r, ACT.Sqrt).then_inc(root_done, 1)

            act.dma_start(square[:, :, :], io["square"].rearrange("p (k n) -> p k n", k=4)).then_inc(square_in, 16)
            act.dma_start(rows[0:int(T_END), :], io["b_in"][0].rearrange("(t n) -> t n", n=P)).then_inc(rows_in, 16)
            act.dma_start(rows[int(T_END):, :], io["norm_mix"][0].rearrange("(t n) -> t n", n=P)).then_inc(rows_in, 16)
            act.dma_start(rel_sb[:, :], io["rel_bias"]).then_inc(table_in, 16)
            act.dma_start(onehot[:, :], io["onehot"]).then_inc(table_in, 16)
            act.dma_start(table[:, :], io["mask"]).then_inc(table_in, 16)
            act.dma_start(bias_rows[:, 0, :], io["b_gate"][0]).then_inc(gu_bias_in, 16)
            act.dma_start(bias_rows[:, 1, :], io["b_up"][0]).then_inc(gu_bias_in, 16)
            act.dma_start(sinks[:, :], io["sinks"].to_broadcast([P, QA])).then_inc(sinks_in, 16)
            b_row = io["b_in"]
            act.dma_start(value_bias[:, 0:KVA * DH], b_row[:, int(T_VA) * P:int(T_QB) * P]).then_inc(sinks_in, 16)
            act.dma_start(value_bias[:, KVA * DH:], b_row[:, int(T_VB) * P:int(T_GA) * P]).then_inc(sinks_in, 16)

            act.wait_ge(x_in, 16)
            for tt in range(TT):
                nc.scalar.activation(h[:, tt, :], x_sb[:, tt, :], ACT.Square,
                                     accum_out=stats[:, tt:tt + 1]).then_inc(sumsq_done, 1)
            root(0)
            act.wait_ge(table_done, 1)
            act.dma_start(scratch, table[:, :]).then_inc(table_out, 16)

            act.wait_ge(columns_done, 1)
            for j, (b, kind, c0, n, t) in enumerate(qkv_jobs):
                act.wait_ge(job_up, j + 1)
                src = bank(PROJ[j % 2])
                if kind == "values":
                    dst = va[:, t, :] if c0 < T_QB * P else vb[:, t, c0 - T_VB * P:c0 - T_VB * P + n]
                    nc.scalar.copy(dst, src[:, 0:n]).then_inc(qkv_copied, 1)
                elif T_KA <= t < T_VA:
                    g = 2 * (t - int(T_KA))
                    for half in range(2):
                        r = slice(half * DH, (half + 1) * DH)
                        last = nc.scalar.activation(kaT[r, g + half, :], src[r, 0:S], ACT.Identity,
                                                    bias=columns[r, t:t + 1])
                    last.then_inc(qkv_copied, 1)
                else:
                    dst = qaT[:, t, :] if t < T_KA else (qbT[:, t - T_QB, :] if t < T_KB else kbT[:, t - T_KB, :])
                    if t < T_KA or T_QB <= t < T_KB:
                        dst = dst[:, ::-1]
                    nc.scalar.activation(dst, src[:, 0:S], ACT.Identity, bias=columns[:, t:t + 1]).then_inc(qkv_copied, 1)

            def copy_turned(n):
                if n >= 2:
                    act.wait_ge(pv_up, n - 1)
                for i, u in enumerate(range(first_unit[n], first_unit[n + 1])):
                    act.wait_ge(turned_up, u + 1)
                    nc.scalar.copy(probsT[:, n % 2, i].rearrange("p a b c -> p (a b c)"),
                                   bank(TURN[u % 2])).then_inc(turned_copied, 1)

            for n, (kind, heads) in enumerate(groups):
                act.wait_ge(peaks_done, n + 1)
                if kind == "A":
                    for i in range(2):
                        for iq in range(2):
                            c = 2 * i + iq
                            v = probs[:, n % 2, i, iq, :]
                            nc.scalar.activation(v, v, ACT.Exp, bias=minus_peak[:, n % 3, c:c + 1],
                                                 accum_out=den[:, n % 3, c:c + 1]).then_inc(exps_done, 1)
                    act.wait_ge(sinks_sub, n + 1)
                    nc.scalar.activation(sink_exp[:, n % 3, :], sink_exp[:, n % 3, :], ACT.Exp).then_inc(sinks_done, 1)
                else:
                    for iq in range(2):
                        v = probs[:, n % 2, :, iq, :]
                        nc.scalar.activation(v, v, ACT.Exp, bias=minus_peak[:, n % 3, iq:iq + 1],
                                             accum_out=den[:, n % 3, iq:iq + 1]).then_inc(exps_done, 2)
                if n >= 1:
                    copy_turned(n - 1)
            copy_turned(len(groups) - 1)
            act.wait_ge(gate_copied, len(gate_jobs))
            for s in range(2):
                v = gates[:, s].rearrange("p f s -> p (f s)")
                nc.scalar.activation(v, v, ACT.Sigmoid).then_inc(gates_done, 1)
            for k in range(5):
                act.wait_ge(mixT_up, k + 1)
                dst = mixT[:, 2 * k:2 * k + 2, :] if k < 4 else mixTb
                nc.scalar.copy(dst[:, :, ::-1], bank(2 + k).rearrange("p (c s) -> p c s", c=2)).then_inc(mixT_done, 1)

            act.wait_ge(merged_done, KC)
            act.wait_ge(out_up, 1)
            act.dma_start(gain_ffn[:, :], io["norm_ffn"].to_broadcast([P, D])).then_inc(moe_in, 16)
            act.dma_start(gain_final[:, :], io["norm_final"].unsqueeze(0).to_broadcast([P, D])).then_inc(moe_in, 16)
            act.dma_start(router[:, :, :], io["router_w"][0].rearrange("(c p) e -> p c e", p=P)).then_inc(moe_in, 16)
            act.dma_start(router_row[:, :], io["router_b"]).then_inc(moe_in, 16)
            act.dma_start(down_bias[:, :], io["b_down"][0]).then_inc(moe_in, 16)
            for tt in range(TT):
                act.wait_ge(x2_done, tt + 1)
                nc.scalar.activation(squares[:, tt, :], x_sb[:, tt, :], ACT.Square,
                                     accum_out=stats[:, 8 + tt:9 + tt]).then_inc(sumsq_done, 1)
            root(1)
            for k in range(4):
                act.wait_ge(h2T_up, k + 1)
                nc.scalar.copy(h2T[:, 2 * k:2 * k + 2, :].rearrange("p c s -> p (c s)"), bank(k)).then_inc(h2T_done, 1)
            for tt in range(TT):
                act.wait_ge(shift_done, 1)
                nc.scalar.activation(weight[:, tt, :], logits[:, tt, :], ACT.Exp,
                                     bias=few[:, tt:tt + 1]).then_inc(exp_done, 1)

            def copy_gathered(it):
                act.wait_ge(gather_up, it + 1)
                nc.scalar.copy(xT[:, :, :].rearrange("p c s -> p (c s)"), bank(GATHER)).then_inc(xT_done, 1)

            act.wait_ge(passes_done, 1)
            n_passes = act.value_load(passes[0:1, 0:1], min_val=1, max_val=PASSES)
            copy_gathered(0)
            with act.Fori(0, n_passes) as p:
                with act.Fori(0, E) as e:
                    it = p * E + e
                    act.wait_ge(gu_used, it * QUADS + 2 * QUADS)
                    nc.scalar.copy(gu[:, 0:BANK], bank(GU)).then_inc(gu_left, 1)
                    copy_gathered(it + 1)
                    act.wait_ge(gate_done, it + 1)
                    nc.scalar.activation(sig[:, :, :], gate_c[:, :, :], ACT.Sigmoid, scale=ALPHA).then_inc(sig_done, 1)
                    act.wait_ge(down_used, it * QUADS + 2 * QUADS)
                    nc.scalar.copy(y_half[:, :], bank(DOWN)).then_inc(y_copied, 1)
            for tt in range(TT):
                act.wait_ge(x2_done, TT + tt + 1)
                nc.scalar.activation(h2[:, tt, :], x_sb[:, tt, :], ACT.Square,
                                     accum_out=stats[:, 16 + tt:17 + tt]).then_inc(sumsq_done, 1)
            root(2)

        @block.tensor
        def _(pe):
            mm, tr = nc.tensor.matmul, nc.tensor.transpose
            pe.wait_ge(square_in, 16)
            pe.wait_ge(rows_in, 32)
            nr = int(T_END) + KC
            tr(bank(0)[:, 0:nr], rows[:, :], ident[0:nr, 0:nr]).then_inc(columns_up, 1)
            pe.wait_ge(table_in, 48)
            mm(bank(1)[0:NU, :], rel_sb[:, :], onehot[:, :], start=True, stop=True).then_inc(table_up, 1)
            pe.wait_ge(gu_bias_in, 32)
            for c in range(KC):
                for j in range(2):
                    last = tr(bank(7)[:, (c * 2 + j) * E:(c * 2 + j + 1) * E], bias_rows[:, j, c * P:(c + 1) * P],
                              ident[0:E, 0:E])
            last.then_inc(gu_bias_up, 1)
            pe.wait_ge(h_done, TT)
            for k in range(4):
                for c in (2 * k, 2 * k + 1):
                    for tt in range(TT):
                        last = tr(bank(2 + k)[:, (c % 2) * S + tt * P:(c % 2) * S + (tt + 1) * P],
                                  h[:, tt, c * P:(c + 1) * P], ident)
                last.then_inc(hT_up, 1)

            def project(j):
                b, kind, c0, n, t = jobs[j]
                first = j == 0 or jobs[j - 1][0] != b
                if first:
                    pe.wait_ge(block_in[b % RING], 16 * (b // RING + 1))
                w = ring_block(b)
                o = bank(PROJ[j % 2])
                lo = c0 - b * W_BLOCK
                if j >= 2:
                    pe.wait_ge(qkv_copied, min(j - 1, len(qkv_jobs)))
                    if j - 1 > len(qkv_jobs):
                        pe.wait_ge(gate_copied, j - 1 - len(qkv_jobs))
                else:
                    pe.wait_ge(columns_done if j == 0 else table_done, 1)
                for c in range(KC):
                    if kind == "turned":
                        last = mm(o[:, 0:S], w[:, c, lo:lo + P], hT[:, c, :], start=c == 0, stop=c == KC - 1)
                    else:
                        mm(o[:, 0:n], hT[:, c, t * P:(t + 1) * P], w[:, c, lo:lo + n], start=c == 0, stop=False)
                if kind == "values":
                    r0 = c0 - T_VA * P if c0 < T_QB * P else KVA * DH + c0 - T_VB * P
                    last = mm(o[:, 0:n], ones[0:1, :], value_bias[0:1, r0:r0 + n], start=False, stop=True)
                last.then_inc(job_up, 1)

            pe.wait_ge(hT_done, KC)
            pe.wait_ge(sinks_in, 48)
            for j in range(len(qkv_jobs)):
                project(j)

            def scores(n):
                kind, heads = groups[n]
                for i, head in enumerate(heads):
                    u = first_unit[n] + i
                    if u >= 2:
                        pe.wait_ge(logits_done, u - 1)
                    if kind == "A":
                        r = slice((head % 2) * DH, (head % 2 + 1) * DH)
                        q, k = qaT[r, head // 2, :], kaT[r, head // (QA // KVA), :]
                    else:
                        hb = n - GA_N
                        r = slice((hb % 2) * DH, (hb % 2 + 1) * DH)
                        q, k = qbT[r, 2 * i + hb // 2, :], kbT[r, 2 * i + hb // 2, :]
                    for iq in range(2):
                        last = mm(bank(SCORE[u % 2])[:, iq * S:(iq + 1) * S], q[:, iq * P:(iq + 1) * P], k,
                                  start=True, stop=True)
                    last.then_inc(scores_up, 1)

            def turn(n):
                pe.wait_ge(exps_done, 4 * (n + 1))
                for i in range(len(groups[n][1])):
                    u = first_unit[n] + i
                    if u >= 2:
                        pe.wait_ge(turned_copied, u - 1)
                    for jt in range(TT):
                        for iq in range(2):
                            at = (jt * 2 + iq) * P
                            last = tr(bank(TURN[u % 2])[:, at:at + P], probs[:, n % 2, i, iq, jt * P:(jt + 1) * P], ident)
                    last.then_inc(turned_up, 1)

            def weigh(n):
                kind, heads = groups[n]
                pe.wait_ge(turned_copied, first_unit[n + 1])
                if n >= 2:
                    pe.wait_ge(mix_done, n - 1)
                for iq in range(2):
                    if kind == "A":
                        for i, head in enumerate(heads):
                            o = bank(PV[n % 2])[:, (iq * 2 + i) * DH:(iq * 2 + i + 1) * DH]
                            kv = head // (QA // KVA)
                            for jt in range(TT):
                                last = mm(o, probsT[:, n % 2, i, jt, iq, :], va[:, jt, kv * DH:(kv + 1) * DH],
                                          start=jt == 0, stop=jt == TT - 1)
                    else:
                        o = bank(PV[n % 2])[:, iq * 2 * DH:iq * 2 * DH + DH]
                        for g in range(NG):
                            col = (g * HB + n - GA_N) * DH
                            for jt in range(TT):
                                last = mm(o, probsT[:, n % 2, g, jt, iq, :], vb[:, jt, col:col + DH],
                                          start=g == 0 and jt == 0, stop=g == NG - 1 and jt == TT - 1)
                last.then_inc(pv_up, 1)

            pe.wait_ge(qkv_copied, len(qkv_jobs))
            pe.wait_ge(keys_done, 1)
            scores(0)
            j = len(qkv_jobs)
            for n in range(len(groups)):
                if n + 1 < len(groups):
                    scores(n + 1)
                for _ in range(2):
                    if j < len(jobs):
                        project(j)
                        j += 1
                turn(n)
                if n >= 1:
                    weigh(n - 1)
            weigh(len(groups) - 1)
            assert j == len(jobs)

            pe.wait_ge(mix_done, len(groups))
            for k in range(5):
                for c in ((2 * k, 2 * k + 1)):
                    for tt in range(TT):
                        last = tr(bank(2 + k)[:, (c % 2) * S + tt * P:(c % 2) * S + (tt + 1) * P],
                                  mix[:, tt, c * P:(c + 1) * P], ident)
                last.then_inc(mixT_up, 1)
            pe.wait_ge(wa_in, 16)
            pe.wait_ge(wb_in, 16)
            pe.wait_ge(mixT_done, 5)
            for f in range(KC):
                pe.wait_ge(gate_copied, len(gate_jobs))
                if f >= 2:
                    pe.wait_ge(products_done, f - 1)
                o = bank(PROJ[f % 2])
                for c in range(KC):
                    mm(o[:, 0:S], wa[:, c, f * P:(f + 1) * P], mixT[:, c, :], start=c == 0, stop=c == KC - 1)
                for c in range(2):
                    last = mm(o[:, S:2 * S], wb[:, c, f * P:(f + 1) * P], mixTb[:, c, :], start=c == 0, stop=c == 1)
                last.then_inc(branch_up, 1)
            pe.wait_ge(wout_in, 16)
            for c in range(KC):
                pe.wait_ge(merged_done, c + 1)
                for tt in range(TT):
                    for nb in range(2):
                        last = mm(bank(2 + 2 * tt + nb), mergedT[:, c, tt * P:(tt + 1) * P],
                                  wout[:, c, nb * BANK:(nb + 1) * BANK], start=c == 0, stop=c == KC - 1)
                if c == 0:
                    last.then_inc(gu_used, QUADS)
            last.then_inc(out_up, 1)

            pe.wait_ge(h2_done, TT)
            for k in range(4):
                for c in (2 * k, 2 * k + 1):
                    for tt in range(TT):
                        last = tr(bank(k)[:, (c % 2) * S + tt * P:(c % 2) * S + (tt + 1) * P],
                                  h2[:, tt, c * P:(c + 1) * P], ident)
                        if c == 0 and tt == 0:
                            last.then_inc(down_used, QUADS)
                last.then_inc(h2T_up, 1)
            pe.wait_ge(moe_in, 80)
            pe.wait_ge(h2T_done, 4)
            for tt in range(TT):
                o = bank(4)[:, tt * E:(tt + 1) * E]
                for c in range(KC):
                    mm(o, h2T[:, c, tt * P:(tt + 1) * P], router[:, c, :], start=c == 0, stop=False)
                last = mm(o, ones[0:1, :], router_row[0:1, :], start=False, stop=True)
            last.then_inc(logits_up, 1)
            pe.wait_ge(chosen_done, 1)
            mm(bank(5)[:, 0:E], tri, chosen[:, 0, :], start=True, stop=True)
            mm(bank(5)[:, E:2 * E], ones, chosen[:, 0, :], start=True, stop=False)
            mm(bank(5)[:, E:2 * E], tri, chosen[:, 1, :], start=False, stop=True)
            mm(bank(5)[:, 2 * E:3 * E], ones, chosen[:, 0, :], start=True, stop=False)
            mm(bank(5)[:, 2 * E:3 * E], ones, chosen[:, 1, :], start=False, stop=True).then_inc(rank_up, 1)
            pe.wait_ge(weight_done, 1)
            for tt in range(TT):
                last = tr(bank(6)[0:E, tt * P:(tt + 1) * P], weight[:, tt, :], ident)
            last.then_inc(weightT_up, 1)
            pe.wait_ge(weightT_done, 1)
            for tt in range(TT):
                for nb in range(2):
                    last = mm(bank(Y + 2 * tt + nb), weightT[:, tt * P:(tt + 1) * P],
                              down_bias[:, nb * BANK:(nb + 1) * BANK], start=True, stop=False, skip_group_check=True)
            last.then_inc(spreadT_up, 1)

            def gather(it):
                pe.wait_ge(pick_done, it + 1)
                for c in range(KC):
                    for tt in range(TT):
                        last = mm(bank(GATHER)[:, c * CAP:(c + 1) * CAP], h2[:, tt, c * P:(c + 1) * P], pick[:, tt, :],
                                  start=tt == 0, stop=tt == TT - 1)
                last.then_inc(gather_up, 1)

            def add_to_tokens(inc=None):
                for tt in range(TT):
                    for half in range(2):
                        r = slice(half * CAP, (half + 1) * CAP)
                        last = mm(bank(Y + 2 * tt + half), spreadT[r, tt * P:(tt + 1) * P], y_half[r, :],
                                  start=False, stop=False, skip_group_check=True)
                return last

            pe.wait_ge(passes_done, 1)
            n_passes = pe.value_load(passes[0:1, 0:1], min_val=1, max_val=PASSES)
            pe.wait_ge(zeroed, 1)
            gather(0)
            with pe.Fori(0, n_passes) as p:
                with pe.Fori(0, E) as e:
                    it = p * E + e
                    pe.wait_ge(xT_done, it + 1)
                    for q in range(QUADS):
                        pe.wait_ge(gate_in[q], 16 * it + 16)
                        pe.wait_ge(up_in[q], 16 * it + 16)
                        for c in range(2):
                            k = 2 * q + c
                            for nb in range(2):
                                cols = slice(nb * BANK, (nb + 1) * BANK)
                                mm(bank(GU + nb)[0:CAP, :], xT[:, k, :], gate_w[q][:, c, cols],
                                   start=k == 0, stop=k == KC - 1)
                                last = mm(bank(GU + nb)[CAP:P, :], xT[:, k, :], up_w[q][:, c, cols],
                                          start=k == 0, stop=k == KC - 1)
                        last.then_inc(gu_used, 1)
                    pe.wait_ge(y_copied, it + 1)
                    add_to_tokens()
                    pe.wait_ge(spread_done, it + 1)
                    for tt in range(TT):
                        last = tr(bank(DOWN)[:, tt * P:(tt + 1) * P], spread[:, tt, :], ident)
                    last.then_inc(spreadT_up, 1)
                    gather(it + 1)
                    pe.wait_ge(gu_left, it + 1)
                    pe.wait_ge(gu_right, it + 1)
                    for c in range(KC):
                        last = tr(bank(GU + c // 4)[:, (c % 4) * P:(c % 4 + 1) * P], gu[:, c * P:(c + 1) * P], ident)
                    last.then_inc(guT_up, 1)
                    pe.wait_ge(spreadT_done, it + 1)
                    pe.wait_ge(hidden_done, it + 1)
                    for q in range(QUADS):
                        pe.wait_ge(down_in[q], 16 * it + 16)
                        for c in range(2):
                            k = 2 * q + c
                            for half in range(2):
                                last = mm(bank(DOWN)[half * CAP:(half + 1) * CAP, :], hidden[:, k, :],
                                          down_w[q][:, c, half * BANK:(half + 1) * BANK], start=k == 0, stop=k == KC - 1)
                        last.then_inc(down_used, 1)
            pe.wait_ge(y_copied, n_passes * E + 1)
            add_to_tokens().then_inc(y_up, 1)

        @block.vector
        def _(dve):
            v = nc.vector
            done, roots = [0], [0]

            def step(ins):
                done[0] += 1
                ins.then_inc(vec, 1)
                dve.wait_ge(vec, done[0])

            def inverse_rms(at, n_sumsq):
                dve.wait_ge(sumsq_done, n_sumsq)
                r = stats[:, at:at + TT]
                step(v.tensor_scalar(r, r, 1.0 / D, EPS, ALU.mult, ALU.add))
                v.reciprocal(r, r).then_inc(inverse_done, 1)
                roots[0] += 1
                dve.wait_ge(root_done, roots[0])

            dve.wait_ge(columns_up, 1)
            v.tensor_copy(columns[:, :], bank(0)[:, 0:int(T_END) + KC]).then_inc(columns_done, 1)
            dve.wait_ge(table_up, 1)
            v.tensor_tensor(table[:, :], table[:, :], bank(1)[0:NU, :], ALU.add).then_inc(table_done, 1)
            dve.wait_ge(gu_bias_up, 1)
            v.tensor_copy(gu_bias[:, :, :, :].rearrange("p e c j -> p (c j) e"),
                          bank(7).rearrange("p (k e) -> p k e", e=E)).then_inc(gu_bias_done, 1)
            inverse_rms(0, TT)
            for tt in range(TT):
                v.tensor_scalar(h[:, tt, :], x_sb[:, tt, :], stats[:, tt:tt + 1], None, ALU.mult).then_inc(h_done, 1)
            for c in range(KC):
                if c % 2 == 0:
                    dve.wait_ge(hT_up, c // 2 + 1)
                g = int(T_END) + c
                v.tensor_scalar(hT[:, c, :], bank(2 + c // 2)[:, (c % 2) * S:(c % 2 + 1) * S], columns[:, g:g + 1], None,
                                ALU.mult).then_inc(hT_done, 1)
            dve.wait_ge(qkv_copied, int(T_VA))
            v.tensor_copy(kaT[DH:P, 0::2, :], kaT[0:DH, 0::2, :])
            v.tensor_copy(kaT[0:DH, 1::2, :], kaT[DH:P, 1::2, :]).then_inc(keys_done, 1)

            def copy_gate(j):
                _, _, _, _, t = gate_jobs[j]
                dve.wait_ge(job_up, len(qkv_jobs) + j + 1)
                f = t - int(T_GA)
                v.tensor_scalar(gates[:, f // KC, f % KC, :], bank(PROJ[(len(qkv_jobs) + j) % 2])[:, 0:S],
                                columns[:, t:t + 1], None, ALU.add).then_inc(gate_copied, 1)

            def logits_of(n):
                kind, heads = groups[n]
                if n >= 2:
                    dve.wait_ge(turned_up, first_unit[n - 1])
                for i in range(len(heads)):
                    u = first_unit[n] + i
                    dve.wait_ge(scores_up, u + 1)
                    dve.wait_ge(window_in[u % BIAS_RING], 16 * (u // BIAS_RING + 1))
                    last = v.scalar_tensor_tensor(probs[:, n % 2, i, :, :], bank(SCORE[u % 2]).rearrange(
                        "p (a b) -> p a b", a=2), SCALE, window(u), ALU.mult, ALU.add)
                    last.then_inc(logits_done, 1)
                dve.wait_ge(logits_done, first_unit[n + 1])
                if kind == "A":
                    step(v.tensor_reduce(peak[:, n % 3, :], probs[:, n % 2, 0:2, :, :].rearrange(
                        "p i q s -> p (i q) s"), AX.X, ALU.max))
                    sk = sinks[:, heads[0]:heads[0] + 2].unsqueeze(2).to_broadcast([P, 2, 2])
                    pk = peak[:, n % 3, :].rearrange("p (i q) -> p i q", i=2)
                    step(v.tensor_tensor(pk, pk, sk, ALU.max))
                    v.tensor_scalar(minus_peak[:, n % 3, :], peak[:, n % 3, :], -1.0, None, ALU.mult).then_inc(peaks_done, 1)
                    v.tensor_tensor(sink_exp[:, n % 3, :].rearrange("p (i q) -> p i q", i=2), sk, pk,
                                    ALU.subtract).then_inc(sinks_sub, 1)
                else:
                    step(v.tensor_reduce(peak[:, n % 3, 0:2], probs[:, n % 2, :, :, :].rearrange(
                        "p i q s -> p q i s"), AX.XY, ALU.max))
                    v.tensor_scalar(minus_peak[:, n % 3, 0:2], peak[:, n % 3, 0:2], -1.0, None,
                                    ALU.mult).then_inc(peaks_done, 1)

            def divide(n):
                kind, heads = groups[n]
                d = den[:, n % 3, :]
                dve.wait_ge(exps_done, 4 * (n + 1))
                if kind == "A":
                    dve.wait_ge(sinks_done, n + 1)
                    step(v.tensor_tensor(d, d, sink_exp[:, n % 3, :], ALU.add))
                    step(v.reciprocal(d, d))
                else:
                    step(v.reciprocal(d[:, 0:2], d[:, 0:2]))
                dve.wait_ge(pv_up, n + 1)
                for iq in range(2):
                    if kind == "A":
                        last = v.tensor_tensor(
                            mix[:, iq, heads[0] * DH:(heads[0] + 2) * DH].rearrange("p (i d) -> p i d", i=2),
                            bank(PV[n % 2])[:, iq * 2 * DH:(iq + 1) * 2 * DH].rearrange("p (i d) -> p i d", i=2),
                            d.rearrange("p (i q) -> p i q", i=2)[:, :, iq:iq + 1].to_broadcast([P, 2, DH]), ALU.mult)
                    else:
                        col = D + (n - GA_N) * DH
                        last = v.tensor_scalar(mix[:, iq, col:col + DH], bank(PV[n % 2])[:, iq * 2 * DH:iq * 2 * DH + DH],
                                               d[:, iq:iq + 1], None, ALU.mult)
                last.then_inc(mix_done, 1)

            logits_of(0)
            j = 0
            for n in range(len(groups)):
                if n + 1 < len(groups):
                    logits_of(n + 1)
                for _ in range(2):
                    if j < len(gate_jobs):
                        copy_gate(j)
                        j += 1
                if n >= 1:
                    divide(n - 1)
            divide(len(groups) - 1)

            dve.wait_ge(gates_done, 2)
            for f in range(KC):
                dve.wait_ge(branch_up, f + 1)
                v.tensor_tensor(products[:, f % 2], gates[:, :, f, :], bank(PROJ[f % 2]).rearrange(
                    "p (j s) -> p j s", j=2), ALU.mult).then_inc(products_done, 1)
                dve.wait_ge(products_done, f + 1)
                v.tensor_tensor(mergedT[:, f, :], products[:, f % 2, 0, :], products[:, f % 2, 1, :],
                                ALU.add).then_inc(merged_done, 1)
            dve.wait_ge(out_up, 1)
            for tt in range(TT):
                v.tensor_tensor(x_sb[:, tt, :], x_sb[:, tt, :], bank(2 + 2 * tt, 2), ALU.add).then_inc(x2_done, 1)
            v.memset(y_half[:, :], 0.0).then_inc(y_copied, 1)
            v.memset(spreadT[:, :], 0.0).then_inc(zeroed, 1)
            v.memset(rank[:, :, :], FAR)
            dve.wait_ge(moe_in, 80)
            inverse_rms(8, 2 * TT)
            for tt in range(TT):
                v.scalar_tensor_tensor(h2[:, tt, :], x_sb[:, tt, :], stats[:, 8 + tt:9 + tt], gain_ffn[:, :],
                                       ALU.mult, ALU.mult).then_inc(h2_done, 1)

            dve.wait_ge(logits_up, 1)
            step(v.tensor_copy(logits[:, :, :], bank(4)[:, 0:TT * E].rearrange("p (t e) -> p t e", t=TT)))
            for tt in range(TT):
                step(v.max(top8[:, tt, :], logits[:, tt, :]))
            v.tensor_scalar(few[:, 0:TT], top8[:, :, 0], -1.0, None, ALU.mult).then_inc(shift_done, 1)
            fourth = top8[:, :, TOPK - 1:TOPK].to_broadcast([P, TT, E])
            v.tensor_tensor(chosen[:, :, :], logits[:, :, :], fourth, ALU.is_gt)
            step(v.tensor_tensor(at_edge[:, :, :], logits[:, :, :], fourth, ALU.is_equal))
            step(v.tensor_reduce(few[:, 2:2 + TT], chosen[:, :, :], AX.X, ALU.add))
            step(v.tensor_scalar(few[:, 2:2 + TT], few[:, 2:2 + TT], -1.0, float(TOPK), ALU.mult, ALU.add))
            for tt in range(TT):
                step(v.tensor_tensor_scan(running[:, tt, :], ones[:, 0:E], at_edge[:, tt, :], 0.0, ALU.mult, ALU.add))
                step(v.tensor_scalar(running[:, tt, :], running[:, tt, :], few[:, 2 + tt:3 + tt], None, ALU.is_le))
            step(v.tensor_tensor(at_edge[:, :, :], at_edge[:, :, :], running[:, :, :], ALU.mult))
            v.tensor_tensor(chosen[:, :, :], chosen[:, :, :], at_edge[:, :, :], ALU.add).then_inc(chosen_done, 1)
            dve.wait_ge(chosen_done, 1)
            dve.wait_ge(exp_done, TT)
            step(v.tensor_tensor(weight[:, :, :], weight[:, :, :], chosen[:, :, :], ALU.mult))
            step(v.tensor_reduce(few[:, 4:4 + TT], weight[:, :, :], AX.X, ALU.add))
            step(v.reciprocal(few[:, 4:4 + TT], few[:, 4:4 + TT]))
            v.tensor_tensor(weight[:, :, :], weight[:, :, :], few[:, 4:4 + TT].unsqueeze(2).to_broadcast([P, TT, E]),
                            ALU.mult).then_inc(weight_done, 1)
            dve.wait_ge(rank_up, 1)
            step(v.tensor_scalar(running[:, :, :], chosen[:, :, :], -FAR, FAR, ALU.mult, ALU.add))
            step(v.tensor_tensor(running[:, :, :], running[:, :, :],
                                 bank(5)[:, 0:TT * E].rearrange("p (t e) -> p t e", t=TT), ALU.add))
            for p in range(PASSES):
                step(v.tensor_scalar(rank[:, :, p * E:(p + 1) * E], running[:, :, :], float(-CAP * p), None, ALU.add))
            step(v.tensor_reduce(few[0:1, 8:9], bank(5)[0:1, 2 * E:3 * E], AX.X, ALU.max))
            for p in range(1, PASSES):
                step(v.tensor_scalar(few[0:1, 8 + p:9 + p], few[0:1, 8:9], float(CAP * p), None, ALU.is_gt))
            step(v.tensor_reduce(few[0:1, 12:13], few[0:1, 9:8 + PASSES], AX.X, ALU.add))
            v.tensor_scalar(passes[:, :], few[0:1, 12:13], 1.0, None, ALU.add).then_inc(passes_done, 1)
            dve.wait_ge(weightT_up, 1)
            v.tensor_copy(weightT[:, :], bank(6)[0:E, 0:S]).then_inc(weightT_done, 1)

            def build_pick(it):
                for tt in range(TT):
                    last = v.tensor_scalar(pick[:, tt, :], slots[:, 0:CAP], rank[:, tt, bass.ds(it, 1)], None, ALU.is_equal)
                last.then_inc(pick_done, 1)

            dve.wait_ge(passes_done, 1)
            n_passes = dve.value_load(passes[0:1, 0:1], min_val=1, max_val=PASSES)
            build_pick(0)
            with dve.Fori(0, n_passes) as p:
                with dve.Fori(0, E) as e:
                    it = p * E + e
                    dve.wait_ge(spreadT_up, it + 1)
                    for tt in range(TT):
                        last = v.tensor_scalar(spread[:, tt, :], slots, rank[:, tt, bass.ds(it, 1)],
                                               weight[:, tt, bass.ds(e, 1)], ALU.is_equal, ALU.mult)
                    last.then_inc(spread_done, 1)
                    dve.wait_ge(gather_up, it + 1)
                    build_pick(it + 1)
                    dve.wait_ge(gu_used, it * QUADS + 2 * QUADS)
                    v.tensor_copy(gu[:, BANK:D], bank(GU + 1)).then_inc(gu_right, 1)
                    dve.wait_ge(spreadT_up, it + 2)
                    v.tensor_copy(spreadT[:, :], bank(DOWN)[:, 0:S]).then_inc(spreadT_done, 1)
                    dve.wait_ge(guT_up, it + 1)
                    v.tensor_tensor(guT[:, :, :, :].rearrange("p c j s -> p (c j) s"),
                                    bank(GU, 2).rearrange("p (k s) -> p k s", s=CAP),
                                    gu_bias[:, bass.ds(e, 1), :, :].rearrange("p o c j -> p (o c j)").unsqueeze(2)
                                    .to_broadcast([P, 2 * KC, CAP]), ALU.add).then_inc(guT_done, 1)
                    dve.wait_ge(guT_done, it + 1)
                    v.tensor_scalar(gate_c[:, :, :], guT[:, :, 0, :], LIMIT, None, ALU.min).then_inc(gate_done, 1)
                    v.tensor_scalar(up_c[:, :, :], guT[:, :, 1, :], -LIMIT, LIMIT, ALU.max, ALU.min).then_inc(up_done, 1)
                    dve.wait_ge(up_done, it + 1)
                    dve.wait_ge(gate_done, it + 1)
                    v.scalar_tensor_tensor(up_c[:, :, :], up_c[:, :, :], 1.0, gate_c[:, :, :], ALU.add,
                                           ALU.mult).then_inc(gated_done, 1)
                    dve.wait_ge(gated_done, it + 1)
                    dve.wait_ge(sig_done, it + 1)
                    v.tensor_tensor(hidden[:, :, :], up_c[:, :, :], sig[:, :, :], ALU.mult).then_inc(hidden_done, 1)

            dve.wait_ge(y_up, 1)
            for tt in range(TT):
                v.tensor_tensor(x_sb[:, tt, :], x_sb[:, tt, :], bank(Y + 2 * tt, 2), ALU.add).then_inc(x2_done, 1)
            inverse_rms(16, 3 * TT)
            for tt in range(TT):
                v.scalar_tensor_tensor(h2[:, tt, :], x_sb[:, tt, :], stats[:, 16 + tt:17 + tt], gain_final[:, :],
                                       ALU.mult, ALU.mult).then_inc(result_done, 1)


INPUTS = ["x", "norm_mix", "w_in", "b_in", "sinks", "rel_bias", "w_branch_a", "w_branch_b", "w_out", "norm_ffn",
          "router_w", "router_b", "w_gate", "b_gate", "w_up", "b_up", "w_down", "b_down", "norm_final"]


def kernel(**inputs):
    import concourse.bacc as bacc
    from concourse.bass_utils import run_bass_kernel_spmd

    nc = bacc.Bacc("TRN2", target_bir_lowering=False, num_devices=1)
    given = {name: np.ascontiguousarray(inputs[name]) for name in INPUTS}
    given.update(constants())
    arrays, io = {}, {}
    for name, a in given.items():
        arrays[f"in_{name}"] = a
        io[name] = nc.dram_tensor(f"in_{name}", a.shape, mybir.dt.from_np(a.dtype), kind="ExternalInput").ap()
    out = nc.dram_tensor("out", (1, S, D), F32, kind="ExternalOutput").ap()
    scratch = nc.dram_tensor("bias_table", (NU, 2 * S), F32, kind="Internal").ap()
    build(nc, io, out, scratch)
    r = run_bass_kernel_spmd(nc, [arrays], core_ids=[0])
    return r.results[0]["out"]
```

```python
from contextlib import ExitStack

import numpy as np

import concourse.bass as bass
from concourse import mybir

F32 = mybir.dt.float32
F32R = mybir.dt.float32r
I32 = mybir.dt.int32
ALU = mybir.AluOpType
ACT = mybir.ActivationFunctionType
AX = mybir.AxisListType

P = 128
BANK = 512
S, D = 256, 1024
TT = S // P
KC = D // P
DH = 64
QA, KVA = 16, 4
HB, NG = 4, 3
DILATION = (1, 4, 16)
B_HALF = 64
A_HALF = 128
NU = QA + HB * NG
BUCKETS, MAX_DISTANCE = 32, 1024
E, TOPK = 32, 4
CAP = 64
PASSES = S // CAP
FAR = 1000.0
LIMIT, ALPHA, EPS, NEG = 7.0, 1.702, 1e-5, -1e30
SCALE = DH ** -0.5

T_QA, T_KA, T_VA, T_QB, T_KB, T_VB, T_GA, T_GB, T_END = np.cumsum(
    [0, QA * DH, KVA * DH, KVA * DH, HB * NG * DH, HB * NG * DH, HB * NG * DH, D, D]) // P
IN_WIDTH = int(T_END) * P

SLOT = 2 * D
PIECE = SLOT // KC
Q_A, K_A, V_A, Q_B, K_B, V_B, GATE_A, GATE_B, W_B = (int(t) * P // PIECE for t in (
    T_QA, T_KA, T_VA, T_QB, T_KB, T_VB, T_GA, T_GB, T_END))
W_A = W_B + 1
W_OUT = W_A + D // PIECE
N_PIECES = W_OUT + D // PIECE
RAW, SPLIT = 5, 3

SLOTS = 12
QUADS = KC // 2


def t5_buckets(rel):
    half = BUCKETS // 2
    exact = half // 2
    n = np.abs(rel)
    large = exact + (np.log(np.maximum(n, 1) / exact) / np.log(MAX_DISTANCE / exact) * (half - exact)).astype(np.int32)
    return (np.where(rel > 0, half, 0) + np.where(n < exact, n, np.minimum(large, half - 1))).astype(np.int32)


def constants():
    square = np.zeros((P, 4 * P), np.float32)
    square[:, 0:P] = np.eye(P)
    square[:, P:2 * P] = np.triu(np.ones((P, P)), 1)
    square[:, 2 * P:3 * P] = 1.0
    square[:, 3 * P:4 * P] = np.arange(P) % CAP
    rel = np.arange(2 * S) - (S - 1)
    onehot = (t5_buckets(rel)[None, :] == np.arange(BUCKETS)[:, None]).astype(np.float32)
    mask = np.zeros((NU, 2 * S), np.float32)
    mask[:QA, np.abs(rel) > A_HALF] = NEG
    for g, d in enumerate(DILATION):
        mask[QA + g * HB:QA + (g + 1) * HB, (rel % d != 0) | (np.abs(rel) > B_HALF * d)] = NEG
    return {"square": square, "onehot": onehot, "mask": mask}


def build(nc, io, out, scratch):
    groups = [("B", [QA + g * HB + h for g in range(NG)]) for h in range(HB)]
    groups += [("A", [2 * n, 2 * n + 1]) for n in range(QA // 2)]
    first_unit = [sum(len(u) for _, u in groups[:n]) for n in range(len(groups) + 1)]
    GROUPS = len(groups)
    N_GATE = W_B - GATE_A

    ctx = ExitStack()

    def sem(name):
        return ctx.enter_context(nc.semaphore(name))

    def area(at):
        here = [at]

        def place(name, shape, dt=F32):
            t = nc.alloc_sbuf_tensor_at(name, shape, dt, offset=here[0])
            here[0] += -(-int(np.prod(shape[1:])) * 4 // 32) * 32
            return t

        return place, here

    with ctx:
        psum = ctx.enter_context(nc.psum_tensor("psum", [P, 8 * BANK], F32))

        def bank(i, n=1):
            return psum[:, i * BANK:(i + n) * BANK]

        base = -(-nc.sbuf_base // 64) * 64
        place, _ = area(base)
        ring = place("ring", [P, SLOTS * SLOT])
        place, _ = area(base)
        raw = place("raw", [P, RAW, SLOT])
        piece_hi = place("piece_hi", [P, SPLIT, SLOT], F32R)
        piece_lo = place("piece_lo", [P, SPLIT, SLOT], F32R)
        hT_lo = place("hT_lo", [P, KC, S], F32R)

        place, here = area(base + SLOTS * SLOT * 4)
        square = place("square_sb", [P, 4, P])
        ident, tri, ones, slots = (square[:, i, :] for i in range(4))
        x_sb = place("x_sb", [P, TT, D])
        columns = place("columns", [P, int(T_END) + KC])
        stats = place("stats", [P, 32])
        few = place("few", [P, 16])

        hT_hi = place("hT_hi", [P, KC, S], F32R)
        at_qk = here[0]
        qaT = place("qaT", [P, QA // 2, S])
        kaT = place("kaT", [P, KVA, S])
        qbT = place("qbT", [P, HB * NG // 2, S])
        kbT = place("kbT", [P, HB * NG // 2, S])
        va = place("va", [P, TT, KVA * DH])
        vb = place("vb", [P, TT, HB * NG * DH])
        gates = place("gates", [P, 2, KC, S])
        end_gates = here[0]
        windows = place("windows", [P, 2, NG, 3 * P])
        at_probs = here[0]
        probs = place("probs", [P, 3, NG, 2, S])
        at_probsT = here[0]
        probsT = place("probsT", [P, 2, NG, TT, 2, P])
        yb = place("yb", [P, TT, HB * DH])
        rows = place("rows", [int(T_END) + KC, P])
        sinks = place("sinks_sb", [P, QA])
        STATS = 5
        peak = place("peak", [P, STATS, 4])
        minus_peak = place("minus_peak", [P, STATS, 4])
        den = place("den", [P, STATS, 4])
        sink_exp = place("sink_exp", [P, STATS, 4])
        assert here[0] <= nc.sbuf_usable_end
        h = gates[:, 0].rearrange("p c s -> p (c s)").rearrange("p (t d) -> p t d", t=TT)
        probs_flat = probs[:, :, :, :, :].rearrange("p a b c d -> p (a b c d)")
        onehot = probs_flat[0:BUCKETS, 0:2 * S]
        table = probs_flat[0:NU, 2 * S:4 * S]
        rel_sb = probs_flat[0:BUCKETS, 4 * S:4 * S + NU]
        value_bias = probsT[0:1].rearrange("p a b c d e -> p (a b c d e)")[:, 0:(KVA + HB * NG) * DH]
        products = windows[:, :, :, :].rearrange("p b i n -> p (b i n)")[:, 0:4 * S].rearrange("p (i n) -> p i n", i=2)
        place, here = area(at_qk)
        mixT_hi = place("mixT_hi", [P, KC + 2, S], F32R)
        mixT_lo = place("mixT_lo", [P, KC + 2, S], F32R)
        place, here = area(at_probs)
        mergedT_hi = place("mergedT_hi", [P, KC, S], F32R)
        mergedT_lo = place("mergedT_lo", [P, KC, S], F32R)

        place, here = area(at_qk - KC * S * 4)
        gu_rows = place("gu_rows", [E, 2, D])
        place, here = area(at_probsT)
        gain_ffn = place("gain_ffn", [P, D])
        down_bias = place("down_bias", [E, D])
        router = place("router", [P, KC, E])
        gu_bias = place("gu_bias", [P, E, KC, 2])
        router_row = place("router_row", [1, E])
        assert here[0] <= at_probsT + 12 * 1024
        place, here = area(at_qk)
        h2 = place("h2", [P, TT, D])
        h2T = place("h2T", [P, KC, S])
        gain_final = place("gain_final", [P, D])
        gu = place("gu", [P, D])
        guT = place("guT", [P, KC, 2, CAP])
        gate_c = place("gate_c", [P, KC, CAP])
        up_c = place("up_c", [P, KC, CAP])
        sig = place("sig", [P, KC, CAP])
        hidden = place("hidden", [P, KC, CAP])
        xT = place("xT", [P, KC, CAP])
        y_half = place("y_half", [P, BANK])
        spreadT = place("spreadT", [P, S])
        spread = place("spread", [P, TT, 2 * CAP])
        pick = place("pick", [P, TT, CAP])
        rank = place("rank", [P, TT, 1 + PASSES * E + 1])
        weight = place("weight", [P, TT, 1 + E])
        logits = place("logits", [P, TT, E])
        top8 = place("top8", [P, TT, 8])
        chosen = place("chosen", [P, TT, E])
        at_edge = place("at_edge", [P, TT, E])
        running = place("running", [P, TT, E])
        weightT = place("weightT", [E, S])
        passes = place("passes", [1, 1], I32)
        assert here[0] <= end_gates
        squares = h2T[:, :, :].rearrange("p (t c) s -> p t (c s)", t=TT)
        weights = weight[:, :, 1:1 + E]

        x_in, square_in, rows_in, table_in, gu_rows_in, sinks_in = (sem(n) for n in (
            "x_in", "square_in", "rows_in", "table_in", "gu_rows_in", "sinks_in"))
        raw_in = [sem(f"raw_in{i}") for i in range(RAW)]
        hi_done, lo_done, piece_up = sem("hi_done"), sem("lo_done"), sem("piece_up")
        sumsq_done, vec, x2_done = sem("sumsq_done"), sem("vec"), sem("x2_done")
        inverse_done, root_done = sem("inverse_done"), sem("root_done")
        h_done, columns_up, columns_done, table_up, table_done = (sem(n) for n in (
            "h_done", "columns_up", "columns_done", "table_up", "table_done"))
        gu_bias_up, gu_bias_done, hT_up, hT_hi_done, hT_lo_done = (sem(n) for n in (
            "gu_bias_up", "gu_bias_done", "hT_up", "hT_hi_done", "hT_lo_done"))
        table_out = sem("table_out")
        window_in = [sem(f"window_in{i}") for i in range(2)]
        qkv_copied, keys_done, gate_copied = (sem(n) for n in ("qkv_copied", "keys_done", "gate_copied"))
        scores_up, logits_done, peaks_done, sinks_sub, exps_done, sinks_done = (sem(n) for n in (
            "scores_up", "logits_done", "peaks_done", "sinks_sub", "exps_done", "sinks_done"))
        turned_up, turned_copied, pv_up, mix_done = (sem(n) for n in (
            "turned_up", "turned_copied", "pv_up", "mix_done"))
        gates_done, mixT_up, mixT_hi_done, mixT_lo_done, branch_b_done = (sem(n) for n in (
            "gates_done", "mixT_up", "mixT_hi_done", "mixT_lo_done", "branch_b_done"))
        products_done, sum_done, merged_hi_done, merged_lo_done = (sem(n) for n in (
            "products_done", "sum_done", "merged_hi_done", "merged_lo_done"))
        x_again, moe_in, gain_in, h2_done, h2T_up, h2T_done, logits_up, shift_done, exp_done = (sem(n) for n in (
            "x_again", "moe_in", "gain_in", "h2_done", "h2T_up", "h2T_done", "logits_up", "shift_done", "exp_done"))
        chosen_done, rank_up, passes_done, weight_done, weightT_up, weightT_done = (sem(n) for n in (
            "chosen_done", "rank_up", "passes_done", "weight_done", "weightT_up", "weightT_done"))
        gate_in = [sem(f"gate_in{i}") for i in range(QUADS)]
        up_in = [sem(f"up_in{i}") for i in range(QUADS)]
        down_in = [sem(f"down_in{i}") for i in range(QUADS)]
        gu_used, down_used = sem("gu_used"), sem("down_used")
        pick_done, spread_done, gather_up, xT_done, spreadT_up, spreadT_done = (sem(n) for n in (
            "pick_done", "spread_done", "gather_up", "xT_done", "spreadT_up", "spreadT_done"))
        gu_left, gu_right, guT_up, guT_done, gate_done, sig_done, up_done, gated_done, hidden_done, y_copied = (
            sem(n) for n in ("gu_left", "gu_right", "guT_up", "guT_done", "gate_done", "sig_done", "up_done",
                             "gated_done", "hidden_done", "y_copied"))
        y_up, result_done, y_out = sem("y_up"), sem("result_done"), sem("y_out")
        block = ctx.enter_context(nc.Block())

        def ring_slot(s):
            return ring[:, s * SLOT:(s + 1) * SLOT].rearrange("p (c n) -> p c n", n=D)

        gate_w = [ring_slot(2 * q) for q in range(QUADS)]
        up_w = [ring_slot(2 * q + 1) for q in range(QUADS)]
        down_w = [ring_slot(8 + q) for q in range(QUADS)]
        PROJ, SCORE, TURN, PV = (0, 1), (2, 3), (4, 5), (6, 7)
        MIX = {4: 2, 0: 3, 1: 0, 2: 1, 3: 2}
        GU_BIAS = 3
        WIDE = 4
        GU, GATHER, DOWN, Y = 0, 2, 3, 4

        def window(n, i):
            w = windows[:, n % 2, i, :]
            return bass.AP(w.tensor, w.offset, [list(w.ap[0]), [P, 2], [1, S]])

        @block.sync
        def _(sp):
            def load_piece(p):
                if p >= RAW:
                    sp.wait_ge(lo_done, p - RAW + 1)
                dst = raw[:, p % RAW, :]
                if p < W_B:
                    src = io["w_in"][0].rearrange("(c p) n -> p c n", p=P)[:, :, p * PIECE:(p + 1) * PIECE]
                elif p == W_B:
                    src = io["w_branch_b"][0].rearrange("(c p) n -> p c n", p=P)
                elif p < W_OUT:
                    n0 = (p - W_A) * PIECE
                    src = io["w_branch_a"][0].rearrange("(c p) n -> p c n", p=P)[:, :, n0:n0 + PIECE]
                else:
                    src = io["w_out"][0].rearrange("(q c p) n -> q p c n", c=2, p=P)[p - W_OUT]
                sp.dma_start(dst.rearrange("p (c n) -> p c n", c=src.shape[1]), src).then_inc(raw_in[p % RAW], 16)

            for tt in range(TT):
                sp.dma_start(x_sb[:, tt, :], io["x"][0, tt * P:(tt + 1) * P, :]).then_inc(x_in, 16)
            sp.dma_start(square[:, :, :], io["square"].rearrange("p (k n) -> p k n", k=4)).then_inc(square_in, 16)
            sp.dma_start(rows[0:int(T_END), :], io["b_in"][0].rearrange("(t n) -> t n", n=P)).then_inc(rows_in, 16)
            sp.dma_start(rows[int(T_END):, :], io["norm_mix"][0].rearrange("(t n) -> t n", n=P)).then_inc(rows_in, 16)
            load_piece(0)
            sp.dma_start(rel_sb, io["rel_bias"]).then_inc(table_in, 16)
            sp.dma_start(onehot, io["onehot"]).then_inc(table_in, 16)
            sp.dma_start(table, io["mask"]).then_inc(table_in, 16)
            load_piece(1)
            sp.dma_start(sinks[:, :], io["sinks"].to_broadcast([P, QA])).then_inc(sinks_in, 16)
            sp.dma_start(value_bias[:, 0:KVA * DH], io["b_in"][:, int(T_VA) * P:int(T_QB) * P]).then_inc(sinks_in, 16)
            sp.dma_start(value_bias[:, KVA * DH:], io["b_in"][:, int(T_VB) * P:int(T_GA) * P]).then_inc(sinks_in, 16)
            for p in range(2, N_PIECES):
                load_piece(p)

            wg = io["w_gate"][0].rearrange("e (q c p) n -> e q p c n", c=2, p=P)
            wu = io["w_up"][0].rearrange("e (q c p) n -> e q p c n", c=2, p=P)
            wd = io["w_down"][0].rearrange("e (q c p) n -> e q p c n", c=2, p=P)

            def load_expert(e, it):
                for q in range(QUADS):
                    sp.wait_ge(gu_used, it * QUADS + q + 1)
                    sp.dma_start(gate_w[q], wg[bass.ds(e, 1), q].rearrange("o p c n -> (o p) c n")).then_inc(gate_in[q], 16)
                    sp.dma_start(up_w[q], wu[bass.ds(e, 1), q].rearrange("o p c n -> (o p) c n")).then_inc(up_in[q], 16)
                for q in range(QUADS):
                    sp.wait_ge(down_used, it * QUADS + q + 1)
                    sp.dma_start(down_w[q], wd[bass.ds(e, 1), q].rearrange("o p c n -> (o p) c n")).then_inc(down_in[q], 16)

            sp.wait_ge(lo_done, N_PIECES)
            with sp.Fori(0, E) as e:
                load_expert(e, e)
            sp.wait_ge(passes_done, 1)
            n = sp.value_load(passes[0:1, 0:1], min_val=1, max_val=PASSES)
            with sp.If(n > 1):
                with sp.Fori(1, n) as p:
                    with sp.Fori(0, E) as e:
                        load_expert(e, p * E + e)
            for tt in range(TT):
                sp.wait_ge(result_done, tt + 1)
                sp.dma_start(out[0, tt * P:(tt + 1) * P, :], h2[:, tt, :]).then_inc(y_out, 16)
            sp.wait_ge(y_out, 16 * TT)

        @block.gpsimd
        def _(pool):
            pool.wait_ge(table_out, 16)
            for n, (_, heads) in enumerate(groups):
                if n >= 2:
                    pool.wait_ge(logits_done, first_unit[n - 1])
                src = bass.AP(scratch.tensor, heads[0] * 2 * S,
                              [[1, P], [(heads[1] - heads[0]) * 2 * S, len(heads)], [1, 3 * P]])
                pool.dma_start(windows[:, n % 2, 0:len(heads), :], src).then_inc(window_in[n % 2], 16)

        @block.scalar
        def _(act):
            def root(k):
                r = stats[:, 8 * k:8 * k + TT]
                act.wait_ge(inverse_done, k + 1)
                nc.scalar.activation(r, r, ACT.Sqrt).then_inc(root_done, 1)

            def split_hi(p):
                if p >= N_PIECES:
                    return
                act.wait_ge(raw_in[p % RAW], 16 * (p // RAW + 1))
                if p >= SPLIT:
                    act.wait_ge(piece_up, p - SPLIT + 1)
                nc.scalar.copy(piece_hi[:, p % SPLIT, :], raw[:, p % RAW, :]).then_inc(hi_done, 1)

            for tt in range(TT):
                act.wait_ge(x_in, 16 * TT)
                nc.scalar.activation(h[:, tt, :], x_sb[:, tt, :], ACT.Square,
                                     accum_out=stats[:, tt:tt + 1]).then_inc(sumsq_done, 1)
            root(0)
            split_hi(0)
            act.wait_ge(columns_done, 1)
            for c in range(KC):
                if c % 2 == 0:
                    act.wait_ge(hT_up, c // 2 + 1)
                g = int(T_END) + c
                nc.scalar.activation(hT_hi[:, c, :], bank(2 + c // 2)[:, (c % 2) * S:(c % 2 + 1) * S], ACT.Copy,
                                     scale=columns[:, g:g + 1]).then_inc(hT_hi_done, 1)
            for p in range(1, SPLIT):
                split_hi(p)
            act.wait_ge(table_done, 1)
            act.dma_start(scratch, table).then_inc(table_out, 16)

            for p in range(GATE_A):
                act.wait_ge(piece_up, p + 1)
                src = bank(PROJ[p % 2]).rearrange("p (k s) -> p k s", k=2)
                if V_A <= p < Q_B or p >= V_B:
                    dst = va[:, :, :] if p < Q_B else vb[:, :, (p - V_B) * PIECE:(p - V_B + 1) * PIECE]
                    nc.scalar.copy(dst, src).then_inc(qkv_copied, 1)
                else:
                    for k in range(2):
                        t = 2 * p + k
                        if K_A <= p < V_A:
                            g = 2 * (t - int(T_KA))
                            for half in range(2):
                                r = slice(half * DH, (half + 1) * DH)
                                last = nc.scalar.activation(kaT[r, g + half, :], src[r, k, :], ACT.Identity,
                                                            bias=columns[r, t:t + 1])
                            continue
                        if p < K_A:
                            dst = qaT[:, t, ::-1]
                        elif p < K_B:
                            dst = qbT[:, t - int(T_QB), ::-1]
                        else:
                            dst = kbT[:, t - int(T_KB), :]
                        last = nc.scalar.activation(dst, src[:, k, :], ACT.Identity, bias=columns[:, t:t + 1])
                    last.then_inc(qkv_copied, 1)
                split_hi(p + SPLIT)

            def copy_turned(n):
                if n >= 2:
                    act.wait_ge(pv_up, n - 1)
                for i, u in enumerate(range(first_unit[n], first_unit[n + 1])):
                    act.wait_ge(turned_up, u + 1)
                    nc.scalar.copy(probsT[:, n % 2, i].rearrange("p a b c -> p (a b c)"),
                                   bank(TURN[u % 2])).then_inc(turned_copied, 1)

            def exps(n):
                kind, heads = groups[n]
                act.wait_ge(peaks_done, n + 1)
                if kind == "A":
                    for i in range(2):
                        for iq in range(2):
                            c = 2 * i + iq
                            v = probs[:, n % 3, i, iq, :]
                            nc.scalar.activation(v, v, ACT.Exp, bias=minus_peak[:, n % STATS, c:c + 1],
                                                 accum_out=den[:, n % STATS, c:c + 1]).then_inc(exps_done, 1)
                    act.wait_ge(sinks_sub, n - HB + 1)
                    v = sink_exp[:, n % STATS, :]
                    nc.scalar.activation(v, v, ACT.Exp).then_inc(sinks_done, 1)
                else:
                    for iq in range(2):
                        v = probs[:, n % 3, :, iq, :]
                        nc.scalar.activation(v, v, ACT.Exp, bias=minus_peak[:, n % STATS, iq:iq + 1],
                                             accum_out=den[:, n % STATS, iq:iq + 1]).then_inc(exps_done, 2)

            exps(0)
            for n in range(GROUPS):
                if n + 1 < GROUPS:
                    exps(n + 1)
                copy_turned(n)
                if n < N_GATE:
                    split_hi(GATE_A + n + SPLIT)
            def mix_hi(i):
                k = list(MIX)[i]
                act.wait_ge(mixT_up, i + 1)
                nc.scalar.copy(mixT_hi[:, 2 * k:2 * k + 2, ::-1],
                               bank(MIX[k]).rearrange("p (c s) -> p c s", c=2)).then_inc(mixT_hi_done, 1)

            def gate(i):
                v = gates[:, i].rearrange("p f s -> p (f s)")
                nc.scalar.activation(v, v, ACT.Sigmoid).then_inc(gates_done, 1)

            for i in range(3):
                mix_hi(i)
            act.wait_ge(pv_up, GROUPS)
            act.dma_start(gu_rows[:, 0, :], io["b_gate"][0]).then_inc(gu_rows_in, 16)
            act.dma_start(gu_rows[:, 1, :], io["b_up"][0]).then_inc(gu_rows_in, 16)
            act.dma_start(gain_ffn[:, :], io["norm_ffn"].to_broadcast([P, D])).then_inc(moe_in, 16)
            act.dma_start(router[:, :, :], io["router_w"][0].rearrange("(c p) e -> p c e", p=P)).then_inc(moe_in, 16)
            act.dma_start(router_row[:, :], io["router_b"]).then_inc(moe_in, 16)
            act.dma_start(down_bias[:, :], io["b_down"][0]).then_inc(moe_in, 16)
            mix_hi(3)
            act.wait_ge(gate_copied, N_GATE)
            gate(1)
            mix_hi(4)
            act.dma_start(x_sb[:, :, :], io["x"][0].rearrange("(t p) d -> p t d", p=P)).then_inc(x_again, 16)
            gate(0)
            act.wait_ge(gu_bias_up, 1)
            nc.scalar.copy(gu_bias[:, :, :, :].rearrange("p e c j -> p (c j) e"),
                           bank(GU_BIAS).rearrange("p (k e) -> p k e", e=E)).then_inc(gu_bias_done, 1)
            split_hi(W_B + SPLIT)
            for m in range(W_OUT - W_A):
                act.wait_ge(sum_done, m + 1)
                nc.scalar.copy(mergedT_hi[:, 2 * m:2 * m + 2, :].rearrange("p c s -> p (c s)"),
                               products[:, m % 2, :]).then_inc(merged_hi_done, 1)
                split_hi(W_A + m + SPLIT)
            split_hi(N_PIECES - 1)

            for tt in range(TT):
                act.wait_ge(x2_done, tt + 1)
                nc.scalar.activation(squares[:, tt, :], x_sb[:, tt, :], ACT.Square,
                                     accum_out=stats[:, 8 + tt:9 + tt]).then_inc(sumsq_done, 1)
            root(1)
            act.dma_start(gain_final[:, :], io["norm_final"].unsqueeze(0).to_broadcast([P, D])).then_inc(gain_in, 16)
            for k in range(4):
                act.wait_ge(h2T_up, k + 1)
                nc.scalar.copy(h2T[:, 2 * k:2 * k + 2, :].rearrange("p c s -> p (c s)"), bank(k)).then_inc(h2T_done, 1)
            for tt in range(TT):
                act.wait_ge(shift_done, 1)
                nc.scalar.activation(weights[:, tt, :], logits[:, tt, :], ACT.Exp,
                                     bias=few[:, tt:tt + 1]).then_inc(exp_done, 1)

            def copy_gathered(it):
                act.wait_ge(gather_up, it + 1)
                nc.scalar.copy(xT[:, :, :].rearrange("p c s -> p (c s)"), bank(GATHER)).then_inc(xT_done, 1)

            act.wait_ge(passes_done, 1)
            n_passes = act.value_load(passes[0:1, 0:1], min_val=1, max_val=PASSES)
            copy_gathered(0)
            with act.Fori(0, n_passes) as p:
                with act.Fori(0, E) as e:
                    it = p * E + e
                    act.wait_ge(gu_used, it * QUADS + 2 * QUADS)
                    nc.scalar.copy(gu[:, 0:BANK], bank(GU)).then_inc(gu_left, 1)
                    act.wait_ge(gate_done, it + 1)
                    nc.scalar.activation(sig[:, :, :], gate_c[:, :, :], ACT.Sigmoid, scale=ALPHA).then_inc(sig_done, 1)
                    copy_gathered(it + 1)
                    act.wait_ge(down_used, it * QUADS + 2 * QUADS)
                    nc.scalar.copy(y_half[:, :], bank(DOWN)).then_inc(y_copied, 1)
            for tt in range(TT):
                act.wait_ge(x2_done, TT + tt + 1)
                nc.scalar.activation(h2[:, tt, :], x_sb[:, tt, :], ACT.Square,
                                     accum_out=stats[:, 16 + tt:17 + tt]).then_inc(sumsq_done, 1)
            root(2)

        @block.tensor
        def _(pe):
            mm, tr = nc.tensor.matmul, nc.tensor.transpose

            def mm3(o, a_hi, a_lo, b_hi, b_lo, first, last):
                mm(o, a_hi, b_hi, start=first, stop=False)
                mm(o, a_hi, b_lo, start=False, stop=False)
                return mm(o, a_lo, b_hi, start=False, stop=last)

            pe.wait_ge(square_in, 16)
            pe.wait_ge(rows_in, 32)
            nr = int(T_END) + KC
            tr(bank(0)[:, 0:nr], rows[:, :], ident[0:nr, 0:nr]).then_inc(columns_up, 1)
            for tt in range(TT):
                pe.wait_ge(h_done, tt + 1)
                for c in range(KC):
                    last = tr(bank(2 + c // 2)[:, (c % 2) * S + tt * P:(c % 2) * S + (tt + 1) * P],
                              h[:, tt, c * P:(c + 1) * P], ident)
                    if tt == TT - 1 and c % 2:
                        last.then_inc(hT_up, 1)
            pe.wait_ge(table_in, 48)
            mm(bank(1)[0:NU, :], rel_sb, onehot, start=True, stop=True).then_inc(table_up, 1)

            def project(p):
                pe.wait_ge(lo_done, p + 1)
                if p == 0:
                    pe.wait_ge(columns_done, 1)
                if p == 1:
                    pe.wait_ge(table_done, 1)
                if p >= 2:
                    pe.wait_ge(qkv_copied, min(p - 1, GATE_A))
                if p - 1 > GATE_A:
                    pe.wait_ge(gate_copied, p - 1 - GATE_A)
                hi = piece_hi[:, p % SPLIT, :].rearrange("p (c n) -> p c n", c=KC)
                lo = piece_lo[:, p % SPLIT, :].rearrange("p (c n) -> p c n", c=KC)
                values = V_A <= p < Q_B or V_B <= p < GATE_A
                for k in range(2):
                    o = bank(PROJ[p % 2])[:, k * S:(k + 1) * S]
                    r = slice(k * P, (k + 1) * P)
                    for c in range(KC):
                        if values:
                            last = mm3(o, hT_hi[:, c, r], hT_lo[:, c, r], hi[:, c, :], lo[:, c, :], c == 0, False)
                        else:
                            last = mm3(o, hi[:, c, r], lo[:, c, r], hT_hi[:, c, :], hT_lo[:, c, :], c == 0, c == KC - 1)
                    if values:
                        pe.wait_ge(sinks_in, 48)
                        r0 = 0 if p < Q_B else (1 + p - V_B) * PIECE
                        last = mm(o, ones[0:1, :], value_bias[0:1, r0:r0 + PIECE], start=False, stop=True)
                last.then_inc(piece_up, 1)

            pe.wait_ge(hT_lo_done, KC)
            for p in range(GATE_A):
                project(p)

            def scores(n, some):
                kind, heads = groups[n]
                for i, head in list(enumerate(heads))[some]:
                    u = first_unit[n] + i
                    if u >= 2:
                        pe.wait_ge(logits_done, u - 1)
                    if kind == "A":
                        r = slice((head % 2) * DH, (head % 2 + 1) * DH)
                        q, k = qaT[r, head // 2, :], kaT[r, head // (QA // KVA), :]
                    else:
                        hb = n
                        r = slice((hb % 2) * DH, (hb % 2 + 1) * DH)
                        q, k = qbT[r, 2 * i + hb // 2, :], kbT[r, 2 * i + hb // 2, :]
                    for iq in range(2):
                        last = mm(bank(SCORE[u % 2])[:, iq * S:(iq + 1) * S], q[:, iq * P:(iq + 1) * P], k,
                                  start=True, stop=True)
                    last.then_inc(scores_up, 1)

            def turn(n):
                pe.wait_ge(exps_done, 4 * (n + 1))
                for i in range(len(groups[n][1])):
                    u = first_unit[n] + i
                    if u >= 2:
                        pe.wait_ge(turned_copied, u - 1)
                    for jt in range(TT):
                        for iq in range(2):
                            at = (jt * 2 + iq) * P
                            last = tr(bank(TURN[u % 2])[:, at:at + P], probs[:, n % 3, i, iq, jt * P:(jt + 1) * P], ident)
                    last.then_inc(turned_up, 1)

            def weigh(n):
                kind, heads = groups[n]
                pe.wait_ge(turned_copied, first_unit[n + 1])
                if n >= 2:
                    pe.wait_ge(mix_done, n - 1)
                for iq in range(2):
                    if kind == "A":
                        for i, head in enumerate(heads):
                            o = bank(PV[n % 2])[:, (iq * 2 + i) * DH:(iq * 2 + i + 1) * DH]
                            kv = head // (QA // KVA)
                            for jt in range(TT):
                                last = mm(o, probsT[:, n % 2, i, jt, iq, :], va[:, jt, kv * DH:(kv + 1) * DH],
                                          start=jt == 0, stop=jt == TT - 1)
                    else:
                        o = bank(PV[n % 2])[:, iq * 2 * DH:iq * 2 * DH + DH]
                        for g in range(NG):
                            col = (g * HB + n) * DH
                            for jt in range(TT):
                                last = mm(o, probsT[:, n % 2, g, jt, iq, :], vb[:, jt, col:col + DH],
                                          start=g == 0 and jt == 0, stop=g == NG - 1 and jt == TT - 1)
                last.then_inc(pv_up, 1)

            def turn_mix(k):
                for c in (2 * k, 2 * k + 1):
                    for tt in range(TT):
                        src = x_sb[:, tt, c * P:(c + 1) * P] if c < KC else yb[:, tt, (c - KC) * P:(c - KC + 1) * P]
                        last = tr(bank(MIX[k])[:, (c % 2) * S + tt * P:(c % 2) * S + (tt + 1) * P], src, ident)
                last.then_inc(mixT_up, 1)

            FIRST, REST = slice(0, 2), slice(2, None)
            pe.wait_ge(qkv_copied, GATE_A)
            pe.wait_ge(keys_done, 1)
            scores(0, FIRST)
            scores(0, REST)
            scores(1, FIRST)
            scores(1, REST)
            for n in range(GROUPS):
                if n + 2 < GROUPS:
                    scores(n + 2, FIRST)
                if n < N_GATE:
                    project(GATE_A + n)
                if n + 2 < GROUPS:
                    scores(n + 2, REST)
                turn(n)
                if n >= 1:
                    weigh(n - 1)
            pe.wait_ge(logits_done, first_unit[GROUPS])
            pe.wait_ge(gate_copied, N_GATE)
            pe.wait_ge(mix_done, HB + 4)
            for k in (4, 0, 1):
                turn_mix(k)
            weigh(GROUPS - 1)
            pe.wait_ge(mix_done, HB + 6)
            turn_mix(2)

            def parts(p, c):
                pe.wait_ge(lo_done, p + 1)
                return (piece_hi[:, p % SPLIT, :].rearrange("p (c n) -> p c n", c=c),
                        piece_lo[:, p % SPLIT, :].rearrange("p (c n) -> p c n", c=c))

            hi, lo = parts(W_B, 2)
            pe.wait_ge(mixT_lo_done, 1)
            for f in range(KC):
                if f == KC // 2:
                    pe.wait_ge(mix_done, GROUPS)
                    turn_mix(3)
                    pe.wait_ge(gu_rows_in, 32)
                    pe.wait_ge(mixT_lo_done, 2)
                    for c in range(KC):
                        for j in range(2):
                            at = (c * 2 + j) * E
                            last = tr(bank(GU_BIAS)[:, at:at + E], gu_rows[:, j, c * P:(c + 1) * P], ident[0:E, 0:E])
                    last.then_inc(gu_bias_up, 1)
                for c in range(2):
                    o = psum[:, WIDE * BANK + f * S:WIDE * BANK + (f + 1) * S]
                    r = slice(f * P, (f + 1) * P)
                    last = mm3(o, hi[:, c, r], lo[:, c, r], mixT_hi[:, KC + c, :], mixT_lo[:, KC + c, :], c == 0, c == 1)
            last.then_inc(piece_up, 1)
            pe.wait_ge(mixT_lo_done, 5)
            for m in range(W_OUT - W_A):
                hi, lo = parts(W_A + m, KC)
                if m >= 2:
                    pe.wait_ge(products_done, m - 1)
                for k in range(2):
                    r = slice(k * P, (k + 1) * P)
                    for c in range(KC):
                        last = mm3(bank(PROJ[m % 2])[:, k * S:(k + 1) * S], hi[:, c, r], lo[:, c, r],
                                   mixT_hi[:, c, :], mixT_lo[:, c, :], c == 0, c == KC - 1)
                last.then_inc(piece_up, 1)
            pe.wait_ge(branch_b_done, 4)
            for m in range(N_PIECES - W_OUT):
                hi, lo = parts(W_OUT + m, 2)
                pe.wait_ge(merged_lo_done, m + 1)
                for k in range(2):
                    c = 2 * m + k
                    for tt in range(TT):
                        r = slice(tt * P, (tt + 1) * P)
                        for nb in range(2):
                            cols = slice(nb * BANK, (nb + 1) * BANK)
                            last = mm3(bank(WIDE + 2 * tt + nb), mergedT_hi[:, c, r], mergedT_lo[:, c, r],
                                       hi[:, k, cols], lo[:, k, cols], c == 0, c == KC - 1)
                        if m == 0 and k == 0 and tt == 0:
                            last.then_inc(gu_used, 2)
                last.then_inc(piece_up, 1)

            pe.wait_ge(h2_done, TT)
            for k in range(4):
                for c in (2 * k, 2 * k + 1):
                    for tt in range(TT):
                        last = tr(bank(k)[:, (c % 2) * S + tt * P:(c % 2) * S + (tt + 1) * P],
                                  h2[:, tt, c * P:(c + 1) * P], ident)
                        if c == 0:
                            last.then_inc(*((gu_used, 2) if tt == 0 else (down_used, QUADS)))
                last.then_inc(h2T_up, 1)
            pe.wait_ge(moe_in, 64)
            for tt in range(TT):
                o = bank(4)[:, tt * E:(tt + 1) * E]
                for c in range(KC):
                    if tt == 0 and c % 2 == 0:
                        pe.wait_ge(h2T_done, c // 2 + 1)
                    mm(o, h2T[:, c, tt * P:(tt + 1) * P], router[:, c, :], start=c == 0, stop=False)
                last = mm(o, ones[0:1, :], router_row[0:1, :], start=False, stop=True)
            last.then_inc(logits_up, 1)
            pe.wait_ge(chosen_done, 1)
            mm(bank(5)[:, 0:E], tri, chosen[:, 0, :], start=True, stop=True)
            mm(bank(5)[:, E:2 * E], ones, chosen[:, 0, :], start=True, stop=False)
            mm(bank(5)[:, E:2 * E], tri, chosen[:, 1, :], start=False, stop=True)
            mm(bank(5)[:, 2 * E:3 * E], ones, chosen[:, 0, :], start=True, stop=False)
            mm(bank(5)[:, 2 * E:3 * E], ones, chosen[:, 1, :], start=False, stop=True).then_inc(rank_up, 1)

            def gather(it):
                pe.wait_ge(pick_done, it + 1)
                for c in range(KC):
                    for tt in range(TT):
                        last = mm(bank(GATHER)[:, c * CAP:(c + 1) * CAP], h2[:, tt, c * P:(c + 1) * P], pick[:, tt, :],
                                  start=tt == 0, stop=tt == TT - 1)
                last.then_inc(gather_up, 1)

            def turn_spread(it):
                pe.wait_ge(spread_done, it + 1)
                for tt in range(TT):
                    last = tr(bank(DOWN)[:, tt * P:(tt + 1) * P], spread[:, tt, :], ident)
                last.then_inc(spreadT_up, 1)

            def add_to_tokens():
                for tt in range(TT):
                    for half in range(2):
                        r = slice(half * CAP, (half + 1) * CAP)
                        last = mm(bank(Y + 2 * tt + half), spreadT[r, tt * P:(tt + 1) * P], y_half[r, :],
                                  start=False, stop=False, skip_group_check=True)
                return last

            gather(0)
            pe.wait_ge(weight_done, 1)
            for tt in range(TT):
                last = tr(bank(6)[0:E, tt * P:(tt + 1) * P], weights[:, tt, :], ident)
            last.then_inc(weightT_up, 1)
            pe.wait_ge(weightT_done, 1)
            for tt in range(TT):
                for nb in range(2):
                    mm(bank(Y + 2 * tt + nb), weightT[:, tt * P:(tt + 1) * P], down_bias[:, nb * BANK:(nb + 1) * BANK],
                       start=True, stop=False, skip_group_check=True)

            pe.wait_ge(passes_done, 1)
            n_passes = pe.value_load(passes[0:1, 0:1], min_val=1, max_val=PASSES)
            with pe.Fori(0, n_passes) as p:
                with pe.Fori(0, E) as e:
                    it = p * E + e
                    pe.wait_ge(xT_done, it + 1)
                    for q in range(QUADS):
                        pe.wait_ge(gate_in[q], 16 * it + 16)
                        pe.wait_ge(up_in[q], 16 * it + 16)
                        for c in range(2):
                            k = 2 * q + c
                            for nb in range(2):
                                cols = slice(nb * BANK, (nb + 1) * BANK)
                                mm(bank(GU + nb)[0:CAP, :], xT[:, k, :], gate_w[q][:, c, cols],
                                   start=k == 0, stop=k == KC - 1)
                                last = mm(bank(GU + nb)[CAP:P, :], xT[:, k, :], up_w[q][:, c, cols],
                                          start=k == 0, stop=k == KC - 1)
                        last.then_inc(gu_used, 1)
                    pe.wait_ge(y_copied, it + 1)
                    turn_spread(it)
                    pe.wait_ge(gu_left, it + 1)
                    pe.wait_ge(gu_right, it + 1)
                    for c in range(KC):
                        last = tr(bank(GU + c // 4)[:, (c % 4) * P:(c % 4 + 1) * P], gu[:, c * P:(c + 1) * P], ident)
                    last.then_inc(guT_up, 1)
                    pe.wait_ge(spreadT_done, it + 1)
                    add_to_tokens()
                    gather(it + 1)
                    pe.wait_ge(hidden_done, it + 1)
                    for q in range(QUADS):
                        pe.wait_ge(down_in[q], 16 * it + 16)
                        for c in range(2):
                            k = 2 * q + c
                            for half in range(2):
                                last = mm(bank(DOWN)[half * CAP:(half + 1) * CAP, :], hidden[:, k, :],
                                          down_w[q][:, c, half * BANK:(half + 1) * BANK], start=k == 0, stop=k == KC - 1)
                        last.then_inc(down_used, 1)
            n_steps = n_passes * E
            pe.wait_ge(y_copied, n_steps + 1)
            turn_spread(n_steps)
            pe.wait_ge(spreadT_done, n_steps + 1)
            add_to_tokens().then_inc(y_up, 1)

        @block.vector
        def _(dve):
            v = nc.vector
            done, roots = [0], [0]

            def step(ins):
                done[0] += 1
                ins.then_inc(vec, 1)
                dve.wait_ge(vec, done[0])

            def inverse_rms(at, n_sumsq):
                dve.wait_ge(sumsq_done, n_sumsq)
                r = stats[:, at:at + TT]
                step(v.tensor_scalar(r, r, 1.0 / D, EPS, ALU.mult, ALU.add))
                v.reciprocal(r, r).then_inc(inverse_done, 1)
                roots[0] += 1
                dve.wait_ge(root_done, roots[0])

            def split_lo(p):
                if p >= N_PIECES:
                    return
                dve.wait_ge(hi_done, p + 1)
                v.tensor_tensor(piece_lo[:, p % SPLIT, :], raw[:, p % RAW, :],
                                piece_hi[:, p % SPLIT, :].bitcast(F32), ALU.subtract).then_inc(lo_done, 1)

            dve.wait_ge(columns_up, 1)
            v.tensor_copy(columns[:, :], bank(0)[:, 0:int(T_END) + KC]).then_inc(columns_done, 1)
            inverse_rms(0, TT)
            for tt in range(TT):
                v.tensor_scalar(h[:, tt, :], x_sb[:, tt, :], stats[:, tt:tt + 1], None, ALU.mult).then_inc(h_done, 1)
            split_lo(0)
            for c in range(KC):
                dve.wait_ge(hT_hi_done, 2 * (c // 2) + 2)
                g = int(T_END) + c
                v.scalar_tensor_tensor(hT_lo[:, c, :], bank(2 + c // 2)[:, (c % 2) * S:(c % 2 + 1) * S],
                                       columns[:, g:g + 1], hT_hi[:, c, :].bitcast(F32), ALU.mult,
                                       ALU.subtract).then_inc(hT_lo_done, 1)
            dve.wait_ge(table_up, 1)
            v.tensor_tensor(table, table, bank(1)[0:NU, :], ALU.add).then_inc(table_done, 1)
            for p in range(1, SPLIT):
                split_lo(p)
            for p in range(GATE_A):
                split_lo(p + SPLIT)
                if p == V_A:
                    dve.wait_ge(qkv_copied, V_A)
                    v.tensor_copy(kaT[DH:P, 0::2, :], kaT[0:DH, 0::2, :])
                    v.tensor_copy(kaT[0:DH, 1::2, :], kaT[DH:P, 1::2, :]).then_inc(keys_done, 1)

            def copy_gates(p):
                dve.wait_ge(piece_up, p + 1)
                for k in range(2):
                    t = 2 * p + k
                    f = t - int(T_GA)
                    last = v.tensor_scalar(gates[:, f // KC, f % KC, :], bank(PROJ[p % 2])[:, k * S:(k + 1) * S],
                                           columns[:, t:t + 1], None, ALU.add)
                last.then_inc(gate_copied, 1)

            def logits_of(n):
                kind, heads = groups[n]
                if n >= 3:
                    dve.wait_ge(turned_up, first_unit[n - 2])
                dve.wait_ge(window_in[n % 2], 16 * (n // 2 + 1))
                for i in range(len(heads)):
                    u = first_unit[n] + i
                    dve.wait_ge(scores_up, u + 1)
                    last = v.scalar_tensor_tensor(probs[:, n % 3, i, :, :], bank(SCORE[u % 2]).rearrange(
                        "p (a b) -> p a b", a=2), SCALE, window(n, i), ALU.mult, ALU.add)
                    last.then_inc(logits_done, 1)
                dve.wait_ge(logits_done, first_unit[n + 1])
                w = n % STATS
                if kind == "A":
                    step(v.tensor_reduce(peak[:, w, :], probs[:, n % 3, 0:2, :, :].rearrange(
                        "p i q s -> p (i q) s"), AX.X, ALU.max))
                    sk = sinks[:, heads[0]:heads[0] + 2].unsqueeze(2).to_broadcast([P, 2, 2])
                    pk = peak[:, w, :].rearrange("p (i q) -> p i q", i=2)
                    step(v.tensor_tensor(pk, pk, sk, ALU.max))
                    v.tensor_scalar(minus_peak[:, w, :], peak[:, w, :], -1.0, None, ALU.mult).then_inc(peaks_done, 1)
                    v.tensor_tensor(sink_exp[:, w, :].rearrange("p (i q) -> p i q", i=2), sk, pk,
                                    ALU.subtract).then_inc(sinks_sub, 1)
                else:
                    step(v.tensor_reduce(peak[:, w, 0:2], probs[:, n % 3, :, :, :].rearrange(
                        "p i q s -> p q i s"), AX.XY, ALU.max))
                    v.tensor_scalar(minus_peak[:, w, 0:2], peak[:, w, 0:2], -1.0, None, ALU.mult).then_inc(peaks_done, 1)

            def divide(n):
                kind, heads = groups[n]
                d = den[:, n % STATS, :]
                dve.wait_ge(exps_done, 4 * (n + 1))
                if kind == "A":
                    dve.wait_ge(sinks_done, n - HB + 1)
                    step(v.tensor_tensor(d, d, sink_exp[:, n % STATS, :], ALU.add))
                    step(v.reciprocal(d, d))
                else:
                    step(v.reciprocal(d[:, 0:2], d[:, 0:2]))
                dve.wait_ge(pv_up, n + 1)
                for iq in range(2):
                    if kind == "A":
                        last = v.tensor_tensor(
                            x_sb[:, iq, heads[0] * DH:(heads[0] + 2) * DH].rearrange("p (i d) -> p i d", i=2),
                            bank(PV[n % 2])[:, iq * 2 * DH:(iq + 1) * 2 * DH].rearrange("p (i d) -> p i d", i=2),
                            d.rearrange("p (i q) -> p i q", i=2)[:, :, iq:iq + 1].to_broadcast([P, 2, DH]), ALU.mult)
                    else:
                        col = n * DH
                        last = v.tensor_scalar(yb[:, iq, col:col + DH], bank(PV[n % 2])[:, iq * 2 * DH:iq * 2 * DH + DH],
                                               d[:, iq:iq + 1], None, ALU.mult)
                last.then_inc(mix_done, 1)

            logits_of(0)
            logits_of(1)
            for n in range(GROUPS):
                if n + 2 < GROUPS:
                    logits_of(n + 2)
                if n < N_GATE:
                    copy_gates(GATE_A + n)
                    split_lo(GATE_A + n + SPLIT)
                if n >= 2:
                    divide(n - 2)
            divide(GROUPS - 2)
            divide(GROUPS - 1)

            for i, k in enumerate(MIX):
                dve.wait_ge(mixT_hi_done, i + 1)
                v.tensor_tensor(mixT_lo[:, 2 * k:2 * k + 2, ::-1], bank(MIX[k]).rearrange("p (c s) -> p c s", c=2),
                                mixT_hi[:, 2 * k:2 * k + 2, ::-1].bitcast(F32), ALU.subtract).then_inc(mixT_lo_done, 1)
            dve.wait_ge(gates_done, 1)
            dve.wait_ge(piece_up, W_B + 1)
            for k in range(4):
                g = gates[:, 1, 2 * k:2 * k + 2, :].rearrange("p f s -> p (f s)")
                v.tensor_tensor(g, g, bank(WIDE + k), ALU.mult).then_inc(branch_b_done, 1)
            split_lo(W_B + SPLIT)
            dve.wait_ge(gates_done, 2)
            for m in range(W_OUT - W_A):
                dve.wait_ge(piece_up, W_A + m + 1)
                if m >= 2:
                    dve.wait_ge(merged_hi_done, m - 1)
                g = gates[:, :, 2 * m:2 * m + 2, :].rearrange("p j f s -> p j (f s)")
                v.tensor_tensor(products[:, m % 2, :], g[:, 0, :], bank(PROJ[m % 2]), ALU.mult).then_inc(products_done, 1)
                dve.wait_ge(products_done, m + 1)
                dve.wait_ge(branch_b_done, 4)
                v.tensor_tensor(products[:, m % 2, :], products[:, m % 2, :], g[:, 1, :], ALU.add).then_inc(sum_done, 1)
                dve.wait_ge(sum_done, m + 1)
                dve.wait_ge(merged_hi_done, m + 1)
                v.tensor_tensor(mergedT_lo[:, 2 * m:2 * m + 2, :].rearrange("p c s -> p (c s)"), products[:, m % 2, :],
                                mergedT_hi[:, 2 * m:2 * m + 2, :].bitcast(F32).rearrange("p c s -> p (c s)"),
                                ALU.subtract).then_inc(merged_lo_done, 1)
                split_lo(W_A + m + SPLIT)
            split_lo(N_PIECES - 1)
            dve.wait_ge(x_again, 16)
            dve.wait_ge(piece_up, N_PIECES)
            for tt in range(TT):
                v.tensor_tensor(x_sb[:, tt, :], x_sb[:, tt, :], bank(WIDE + 2 * tt, 2), ALU.add).then_inc(x2_done, 1)
            v.memset(rank[:, :, :], FAR)
            v.memset(y_half[:, :], 0.0).then_inc(y_copied, 1)
            dve.wait_ge(moe_in, 64)
            inverse_rms(8, 2 * TT)
            for tt in range(TT):
                v.scalar_tensor_tensor(h2[:, tt, :], x_sb[:, tt, :], stats[:, 8 + tt:9 + tt], gain_ffn[:, :],
                                       ALU.mult, ALU.mult).then_inc(h2_done, 1)

            dve.wait_ge(logits_up, 1)
            step(v.tensor_copy(logits[:, :, :], bank(4)[:, 0:TT * E].rearrange("p (t e) -> p t e", t=TT)))
            for tt in range(TT):
                step(v.max(top8[:, tt, :], logits[:, tt, :]))
            fourth = top8[:, :, TOPK - 1:TOPK].to_broadcast([P, TT, E])
            v.tensor_tensor(chosen[:, :, :], logits[:, :, :], fourth, ALU.is_gt)
            step(v.tensor_tensor(at_edge[:, :, :], logits[:, :, :], fourth, ALU.is_equal))
            step(v.tensor_reduce(few[:, 2:2 + TT], chosen[:, :, :], AX.X, ALU.add))
            step(v.tensor_scalar(few[:, 2:2 + TT], few[:, 2:2 + TT], -1.0, float(TOPK), ALU.mult, ALU.add))
            for tt in range(TT):
                step(v.tensor_tensor_scan(running[:, tt, :], ones[:, 0:E], at_edge[:, tt, :], 0.0, ALU.mult, ALU.add))
                step(v.tensor_scalar(running[:, tt, :], running[:, tt, :], few[:, 2 + tt:3 + tt], None, ALU.is_le))
            step(v.tensor_tensor(at_edge[:, :, :], at_edge[:, :, :], running[:, :, :], ALU.mult))
            v.tensor_tensor(chosen[:, :, :], chosen[:, :, :], at_edge[:, :, :], ALU.add).then_inc(chosen_done, 1)
            v.tensor_scalar(few[:, 0:TT], top8[:, :, 0], -1.0, None, ALU.mult).then_inc(shift_done, 1)
            dve.wait_ge(chosen_done, 1)
            step(v.tensor_scalar(running[:, :, :], chosen[:, :, :], -FAR, FAR, ALU.mult, ALU.add))
            dve.wait_ge(rank_up, 1)
            step(v.tensor_tensor(running[:, :, :], running[:, :, :],
                                 bank(5)[:, 0:TT * E].rearrange("p (t e) -> p t e", t=TT), ALU.add))
            for p in range(PASSES):
                step(v.tensor_scalar(rank[:, :, 1 + p * E:1 + (p + 1) * E], running[:, :, :], float(-CAP * p), None,
                                     ALU.add))

            def build_pick(it):
                for tt in range(TT):
                    last = v.tensor_scalar(pick[:, tt, :], slots[:, 0:CAP], rank[:, tt, bass.ds(it + 1, 1)], None,
                                           ALU.is_equal)
                last.then_inc(pick_done, 1)

            def build_spread(it, e):
                for tt in range(TT):
                    last = v.tensor_scalar(spread[:, tt, :], slots, rank[:, tt, bass.ds(it, 1)],
                                           weight[:, tt, bass.ds(e, 1)], ALU.is_equal, ALU.mult)
                last.then_inc(spread_done, 1)

            build_pick(0)
            dve.wait_ge(exp_done, TT)
            step(v.tensor_tensor(weights, weights, chosen[:, :, :], ALU.mult))
            step(v.tensor_reduce(few[:, 4:4 + TT], weights, AX.X, ALU.add))
            step(v.reciprocal(few[:, 4:4 + TT], few[:, 4:4 + TT]))
            v.tensor_tensor(weights, weights, few[:, 4:4 + TT].unsqueeze(2).to_broadcast([P, TT, E]),
                            ALU.mult).then_inc(weight_done, 1)
            dve.wait_ge(weight_done, 1)
            step(v.tensor_copy(weight[:, :, 0:1], weight[:, :, E:E + 1]))
            step(v.tensor_reduce(few[0:1, 8:9], bank(5)[0:1, 2 * E:3 * E], AX.X, ALU.max))
            for p in range(1, PASSES):
                step(v.tensor_scalar(few[0:1, 8 + p:9 + p], few[0:1, 8:9], float(CAP * p), None, ALU.is_gt))
            step(v.tensor_reduce(few[0:1, 12:13], few[0:1, 9:8 + PASSES], AX.X, ALU.add))
            v.tensor_scalar(passes[:, :], few[0:1, 12:13], 1.0, None, ALU.add).then_inc(passes_done, 1)
            dve.wait_ge(weightT_up, 1)
            v.tensor_copy(weightT[:, :], bank(6)[0:E, 0:S]).then_inc(weightT_done, 1)

            dve.wait_ge(passes_done, 1)
            n_passes = dve.value_load(passes[0:1, 0:1], min_val=1, max_val=PASSES)
            build_spread(0, 0)
            with dve.Fori(0, n_passes) as p:
                with dve.Fori(0, E) as e:
                    it = p * E + e
                    dve.wait_ge(gather_up, it + 1)
                    build_pick(it + 1)
                    dve.wait_ge(gu_used, it * QUADS + 2 * QUADS)
                    v.tensor_copy(gu[:, BANK:D], bank(GU + 1)).then_inc(gu_right, 1)
                    dve.wait_ge(spreadT_up, it + 1)
                    v.tensor_copy(spreadT[:, :], bank(DOWN)[:, 0:S]).then_inc(spreadT_done, 1)
                    dve.wait_ge(guT_up, it + 1)
                    v.tensor_tensor(guT[:, :, :, :].rearrange("p c j s -> p (c j) s"),
                                    bank(GU, 2).rearrange("p (k s) -> p k s", s=CAP),
                                    gu_bias[:, bass.ds(e, 1), :, :].rearrange("p o c j -> p (o c j)").unsqueeze(2)
                                    .to_broadcast([P, 2 * KC, CAP]), ALU.add).then_inc(guT_done, 1)
                    dve.wait_ge(guT_done, it + 1)
                    v.tensor_scalar(gate_c[:, :, :], guT[:, :, 0, :], LIMIT, None, ALU.min).then_inc(gate_done, 1)
                    v.tensor_scalar(up_c[:, :, :], guT[:, :, 1, :], -LIMIT, LIMIT, ALU.max, ALU.min).then_inc(up_done, 1)
                    dve.wait_ge(up_done, it + 1)
                    dve.wait_ge(gate_done, it + 1)
                    v.scalar_tensor_tensor(up_c[:, :, :], up_c[:, :, :], 1.0, gate_c[:, :, :], ALU.add,
                                           ALU.mult).then_inc(gated_done, 1)
                    dve.wait_ge(gated_done, it + 1)
                    dve.wait_ge(sig_done, it + 1)
                    v.tensor_tensor(hidden[:, :, :], up_c[:, :, :], sig[:, :, :], ALU.mult).then_inc(hidden_done, 1)
                    build_spread(it + 1, e + 1)
            n_steps = n_passes * E
            dve.wait_ge(spreadT_up, n_steps + 1)
            v.tensor_copy(spreadT[:, :], bank(DOWN)[:, 0:S]).then_inc(spreadT_done, 1)

            dve.wait_ge(y_up, 1)
            for tt in range(TT):
                v.tensor_tensor(x_sb[:, tt, :], x_sb[:, tt, :], bank(Y + 2 * tt, 2), ALU.add).then_inc(x2_done, 1)
            dve.wait_ge(gain_in, 16)
            inverse_rms(16, 3 * TT)
            for tt in range(TT):
                v.scalar_tensor_tensor(h2[:, tt, :], x_sb[:, tt, :], stats[:, 16 + tt:17 + tt], gain_final[:, :],
                                       ALU.mult, ALU.mult).then_inc(result_done, 1)


INPUTS = ["x", "norm_mix", "w_in", "b_in", "sinks", "rel_bias", "w_branch_a", "w_branch_b", "w_out", "norm_ffn",
          "router_w", "router_b", "w_gate", "b_gate", "w_up", "b_up", "w_down", "b_down", "norm_final"]


def kernel(**inputs):
    import concourse.bacc as bacc
    from concourse.bass_utils import run_bass_kernel_spmd

    nc = bacc.Bacc("TRN2", target_bir_lowering=False, num_devices=1)
    given = {name: np.ascontiguousarray(inputs[name]) for name in INPUTS}
    given.update(constants())
    arrays, io = {}, {}
    for name, a in given.items():
        arrays[f"in_{name}"] = a
        io[name] = nc.dram_tensor(f"in_{name}", a.shape, mybir.dt.from_np(a.dtype), kind="ExternalInput").ap()
    out = nc.dram_tensor("out", (1, S, D), F32, kind="ExternalOutput").ap()
    scratch = nc.dram_tensor("bias_table", (NU, 2 * S), F32, kind="Internal").ap()
    build(nc, io, out, scratch)
    r = run_bass_kernel_spmd(nc, [arrays], core_ids=[0])
    return r.results[0]["out"]
```

```python
from contextlib import ExitStack

import numpy as np

import concourse.bass as bass
from concourse import mybir

F32 = mybir.dt.float32
F32R = mybir.dt.float32r
I32 = mybir.dt.int32
ALU = mybir.AluOpType
ACT = mybir.ActivationFunctionType
AX = mybir.AxisListType

P = 128
BANK = 512
S, D = 256, 1024
TT = S // P
KC = D // P
DH = 64
QA, KVA = 16, 4
HB, NG = 4, 3
DILATION = (1, 4, 16)
B_HALF = 64
A_HALF = 128
NU = QA + HB * NG
BUCKETS, MAX_DISTANCE = 32, 1024
E, TOPK = 32, 4
CAP = 64
PASSES = S // CAP
FAR = 1000.0
LIMIT, ALPHA, EPS, NEG = 7.0, 1.702, 1e-5, -1e30
SCALE = DH ** -0.5

T_QA, T_KA, T_VA, T_QB, T_KB, T_VB, T_GA, T_GB, T_END = np.cumsum(
    [0, QA * DH, KVA * DH, KVA * DH, HB * NG * DH, HB * NG * DH, HB * NG * DH, D, D]) // P
IN_WIDTH = int(T_END) * P

SLOT = 2 * D
PIECE = SLOT // KC
Q_A, K_A, V_A, Q_B, K_B, V_B, GATE_A, GATE_B, W_B = (int(t) * P // PIECE for t in (
    T_QA, T_KA, T_VA, T_QB, T_KB, T_VB, T_GA, T_GB, T_END))
W_A = W_B + 1
W_OUT = W_A + D // PIECE
N_PIECES = W_OUT + D // PIECE
RAW, SPLIT = 5, 3

QUADS = KC // 2


def t5_buckets(rel):
    half = BUCKETS // 2
    exact = half // 2
    n = np.abs(rel)
    large = exact + (np.log(np.maximum(n, 1) / exact) / np.log(MAX_DISTANCE / exact) * (half - exact)).astype(np.int32)
    return (np.where(rel > 0, half, 0) + np.where(n < exact, n, np.minimum(large, half - 1))).astype(np.int32)


def constants():
    square = np.zeros((P, 4 * P), np.float32)
    square[:, 0:P] = np.eye(P)
    square[:, P:2 * P] = np.triu(np.ones((P, P)), 1)
    square[:, 2 * P:3 * P] = 1.0
    square[:, 3 * P:4 * P] = np.arange(P) % CAP
    rel = np.arange(2 * S) - (S - 1)
    onehot = (t5_buckets(rel)[None, :] == np.arange(BUCKETS)[:, None]).astype(np.float32)
    mask = np.zeros((NU, 2 * S), np.float32)
    mask[:QA, np.abs(rel) > A_HALF] = NEG
    for g, d in enumerate(DILATION):
        mask[QA + g * HB:QA + (g + 1) * HB, (rel % d != 0) | (np.abs(rel) > B_HALF * d)] = NEG
    return {"square": square, "onehot": onehot, "mask": mask}


def build(nc, io, out, scratch):
    groups = [("B", [QA + g * HB + h for g in range(NG)]) for h in range(HB)]
    groups += [("A", [2 * n, 2 * n + 1]) for n in range(QA // 2)]
    first_unit = [sum(len(u) for _, u in groups[:n]) for n in range(len(groups) + 1)]
    GROUPS = len(groups)
    N_GATE = W_B - GATE_A

    ctx = ExitStack()

    def sem(name):
        return ctx.enter_context(nc.semaphore(name))

    def area(at):
        here = [at]

        def place(name, shape, dt=F32):
            t = nc.alloc_sbuf_tensor_at(name, shape, dt, offset=here[0])
            here[0] += -(-int(np.prod(shape[1:])) * 4 // 32) * 32
            return t

        return place, here

    with ctx:
        psum = ctx.enter_context(nc.psum_tensor("psum", [P, 8 * BANK], F32))

        def bank(i, n=1):
            return psum[:, i * BANK:(i + n) * BANK]

        base = -(-nc.sbuf_base // 64) * 64
        place, here = area(base)
        raw = place("raw", [P, RAW, SLOT])
        piece_hi = place("piece_hi", [P, SPLIT, SLOT], F32R)
        piece_lo = place("piece_lo", [P, SPLIT, SLOT], F32R)
        hT_lo = place("hT_lo", [P, KC, S], F32R)

        square = place("square_sb", [P, 4, P])
        ident, tri, ones, slots = (square[:, i, :] for i in range(4))
        at_x = here[0]
        x_sb = place("x_sb", [P, TT, D])
        columns = place("columns", [P, int(T_END) + KC])
        stats = place("stats", [P, 32])
        few = place("few", [P, 16])
        one = place("one", [P, 1])
        unused = place("unused", [P, 4])

        at_hT = here[0]
        hT_hi = place("hT_hi", [P, KC, S], F32R)
        at_qk = here[0]
        qaT = place("qaT", [P, QA // 2, S])
        kaT = place("kaT", [P, KVA, S])
        qbT = place("qbT", [P, HB * NG // 2, S])
        kbT = place("kbT", [P, HB * NG // 2, S])
        va = place("va", [P, TT, KVA * DH])
        vb = place("vb", [P, TT, HB * NG * DH])
        at_gates = here[0]
        gates = place("gates", [P, 2, KC, S])
        windows = place("windows", [P, 2, NG, 3 * P])
        at_probs = here[0]
        probs = place("probs", [P, 3, NG, 2, S])
        at_probsT = here[0]
        probsT = place("probsT", [P, 2, NG, TT, 2, P])
        yb = place("yb", [P, TT, HB * DH])
        rows = place("rows", [int(T_END) + KC, P])
        sinks = place("sinks_sb", [P, QA])
        STATS = 5
        peak = place("peak", [P, STATS, 4])
        minus_peak = place("minus_peak", [P, STATS, 4])
        den = place("den", [P, STATS, 4])
        sink_exp = place("sink_exp", [P, STATS, 4])
        assert here[0] <= nc.sbuf_usable_end
        h = gates[:, 0].rearrange("p c s -> p (c s)").rearrange("p (t d) -> p t d", t=TT)
        probs_flat = probs[:, :, :, :, :].rearrange("p a b c d -> p (a b c d)")
        onehot = probs_flat[0:BUCKETS, 0:2 * S]
        table = probs_flat[0:NU, 2 * S:4 * S]
        rel_sb = probs_flat[0:BUCKETS, 4 * S:4 * S + NU]
        value_bias = probsT[0:1].rearrange("p a b c d e -> p (a b c d e)")[:, 0:(KVA + HB * NG) * DH]
        products = windows[:, :, :, :].rearrange("p b i n -> p (b i n)")[:, 0:4 * S].rearrange("p (i n) -> p i n", i=2)
        place, here = area(at_qk)
        mixT_hi = place("mixT_hi", [P, KC + 2, S], F32R)
        mixT_lo = place("mixT_lo", [P, KC + 2, S], F32R)
        after_mixT = here[0]
        place, here = area(at_probs)
        mergedT_hi = place("mergedT_hi", [P, KC, S], F32R)
        mergedT_lo = place("mergedT_lo", [P, KC, S], F32R)

        place, here = area(after_mixT)
        gu_rows = place("gu_rows", [E, 2, D])
        at_bias = here[0]
        down_bias = place("down_bias", [E, D])
        assert here[0] <= at_gates
        place, here = area(at_probsT)
        gu_bias = place("gu_bias", [P, E, KC, 2])
        at_router = here[0]
        gain_ffn = place("gain_ffn", [P, D])
        router = place("router", [P, KC, E])
        router_row = place("router_row", [1, E])
        late_slot = (nc.sbuf_usable_end - SLOT * 4) // 32 * 32
        assert max(here[0], at_router + SLOT * 4) <= late_slot
        place, here = area(at_qk)
        h2 = place("h2", [P, TT, D])
        at_h2T = here[0]
        h2T = place("h2T", [P, KC, S])
        gain_final = place("gain_final", [P, D])
        gu = place("gu", [P, D])
        xT = place("xT", [P, KC, CAP])
        rank = place("rank", [P, TT, PASSES * E + 1])
        pick = place("pick", [P, TT, CAP])
        logits = place("logits", [P, TT, E])
        assert here[0] <= at_bias
        place, here = area(at_gates)
        guT = place("guT", [P, KC, 2, CAP])
        gate_c = place("gate_c", [P, KC, CAP])
        up_c = place("up_c", [P, KC, CAP])
        sig = place("sig", [P, KC, CAP])
        hidden = place("hidden", [P, KC, CAP])
        y_half = place("y_half", [P, BANK])
        spreadT = place("spreadT", [P, S])
        spread = place("spread", [P, TT, 2 * CAP])
        top8 = place("top8", [P, TT, 8])
        chosen = place("chosen", [P, TT, E])
        at_edge = place("at_edge", [P, TT, E])
        running = place("running", [P, TT, E])
        weights = place("weights", [P, TT, E])
        weightT = place("weightT", [E, S])
        further = place("further", [1, 1], I32)
        at_last = here[0]
        squares = h2T[:, :, :].rearrange("p (t c) s -> p t (c s)", t=TT)

        at_raw, at_hi = base, base + RAW * SLOT * 4
        at_lo = at_hi + SPLIT * SLOT * 4
        last_raw = [(N_PIECES - RAW + i) % RAW for i in range(RAW)]
        last_split = [(N_PIECES - SPLIT + i) % SPLIT for i in range(SPLIT)]
        slot_places = [at_lo + SPLIT * SLOT * 4, at_hT, late_slot]
        slot_places += [at_raw + i * SLOT * 4 for i in last_raw] + [at_x]
        slot_places += [at + i * SLOT * 4 for i in last_split for at in (at_hi, at_lo)]
        slot_places += [at_last + i * SLOT * 4 for i in range(3)] + [at_router, at_h2T]
        assert at_last + 3 * SLOT * 4 <= at_probsT and len(slot_places) == 5 * QUADS
        slot = [nc.alloc_sbuf_tensor_at(f"slot{i}", [P, 2, D], F32, offset=at) for i, at in enumerate(slot_places)]

        square_in, rows_in, table_in, gu_rows_in, sinks_in = (sem(n) for n in (
            "square_in", "rows_in", "table_in", "gu_rows_in", "sinks_in"))
        x_in = [sem(f"x_in{tt}") for tt in range(TT)]
        one_done = sem("one_done")
        raw_in = [sem(f"raw_in{i}") for i in range(RAW)]
        hi_done, lo_done, piece_up = sem("hi_done"), sem("lo_done"), sem("piece_up")
        sumsq_done, vec, x2_up = sem("sumsq_done"), sem("vec"), sem("x2_up")
        inverse_done, root_done = sem("inverse_done"), sem("root_done")
        h_done, columns_up, columns_done, table_up, table_done = (sem(n) for n in (
            "h_done", "columns_up", "columns_done", "table_up", "table_done"))
        gu_bias_up, gu_bias_done, hT_up, hT_hi_done, hT_lo_done = (sem(n) for n in (
            "gu_bias_up", "gu_bias_done", "hT_up", "hT_hi_done", "hT_lo_done"))
        table_out = sem("table_out")
        window_in = [sem(f"window_in{i}") for i in range(2)]
        qkv_copied, keys_done, gate_copied = (sem(n) for n in ("qkv_copied", "keys_done", "gate_copied"))
        scores_up, logits_done, peaks_done, sinks_sub, exps_done, sinks_done = (sem(n) for n in (
            "scores_up", "logits_done", "peaks_done", "sinks_sub", "exps_done", "sinks_done"))
        turned_up, turned_copied, pv_up, mix_done = (sem(n) for n in (
            "turned_up", "turned_copied", "pv_up", "mix_done"))
        gates_done, mixT_up, mixT_hi_done, mixT_lo_done, branch_b_done = (sem(n) for n in (
            "gates_done", "mixT_up", "mixT_hi_done", "mixT_lo_done", "branch_b_done"))
        products_done, sum_done, merged_hi_done, merged_lo_done = (sem(n) for n in (
            "products_done", "sum_done", "merged_hi_done", "merged_lo_done"))
        x_again, moe_in, gain_in, h2_done, h2T_up, h2T_left, h2T_right, logits_up, shift_done, exp_done = (sem(n) for n in (
            "x_again", "moe_in", "gain_in", "h2_done", "h2T_up", "h2T_left", "h2T_right", "logits_up", "shift_done", "exp_done"))
        chosen_done, rank_up, passes_done, weight_done, weightT_up, weightT_done = (sem(n) for n in (
            "chosen_done", "rank_up", "passes_done", "weight_done", "weightT_up", "weightT_done"))
        gate_in = [[sem(f"gate_in{b}_{q}") for q in range(QUADS)] for b in range(2)]
        up_in = [[sem(f"up_in{b}_{q}") for q in range(QUADS)] for b in range(2)]
        down_in = [sem(f"down_in{i}") for i in range(QUADS)]
        first_in = [sem(f"first_in{i}") for i in range(3 * QUADS)]
        gather_half, xT_half, gu_half = sem("gather_half"), sem("xT_half"), sem("gu_half")
        gu_used, down_used = sem("gu_used"), sem("down_used")
        pick_done, spread_done, gather_up, xT_done, spreadT_up, spreadT_done = (sem(n) for n in (
            "pick_done", "spread_done", "gather_up", "xT_done", "spreadT_up", "spreadT_done"))
        gu_left, gu_right, guT_up, guT_done, gate_done, sig_done, up_done, gated_done, hidden_done, y_copied = (
            sem(n) for n in ("gu_left", "gu_right", "guT_up", "guT_done", "gate_done", "sig_done", "up_done",
                             "gated_done", "hidden_done", "y_copied"))
        y_up, result_done, y_out = sem("y_up"), sem("result_done"), sem("y_out")
        block = ctx.enter_context(nc.Block())

        down_w, even, odd = slot[:QUADS], slot[QUADS:3 * QUADS], slot[3 * QUADS:]
        gate_w = [[own[2 * q] for q in range(QUADS)] for own in (even, odd)]
        up_w = [[own[2 * q + 1] for q in range(QUADS)] for own in (even, odd)]

        PROJ, SCORE, TURN, PV = (0, 1), (2, 3), (4, 5), (6, 7)
        MIX = {4: 2, 0: 3, 1: 0, 2: 1, 3: 2}
        GU_BIAS, COLUMNS, TABLE = 3, 6, 7
        WIDE = 4
        GU, GATHER, DOWN, Y = 0, 2, 3, 4
        LOGITS, RANKS = 0, 1

        def window(n, i):
            w = windows[:, n % 2, i, :]
            return bass.AP(w.tensor, w.offset, [list(w.ap[0]), [P, 2], [1, S]])

        @block.sync
        def _(sp):
            def load_piece(p):
                if p >= RAW:
                    sp.wait_ge(lo_done, p - RAW + 1)
                dst = raw[:, p % RAW, :]
                if p < W_B:
                    src = io["w_in"][0].rearrange("(c p) n -> p c n", p=P)[:, :, p * PIECE:(p + 1) * PIECE]
                elif p == W_B:
                    src = io["w_branch_b"][0].rearrange("(c p) n -> p c n", p=P)
                elif p < W_OUT:
                    n0 = (p - W_A) * PIECE
                    src = io["w_branch_a"][0].rearrange("(c p) n -> p c n", p=P)[:, :, n0:n0 + PIECE]
                else:
                    src = io["w_out"][0].rearrange("(q c p) n -> q p c n", c=2, p=P)[p - W_OUT]
                sp.dma_start(dst.rearrange("p (c n) -> p c n", c=src.shape[1]), src).then_inc(raw_in[p % RAW], 16)

            for tt in range(TT):
                sp.dma_start(x_sb[:, tt, :], io["x"][0, tt * P:(tt + 1) * P, :]).then_inc(x_in[tt], 16)
            sp.dma_start(square[:, :, :], io["square"].rearrange("p (k n) -> p k n", k=4)).then_inc(square_in, 16)
            sp.dma_start(rows[0:int(T_END), :], io["b_in"][0].rearrange("(t n) -> t n", n=P)).then_inc(rows_in, 16)
            sp.dma_start(rows[int(T_END):, :], io["norm_mix"][0].rearrange("(t n) -> t n", n=P)).then_inc(rows_in, 16)
            load_piece(0)
            sp.dma_start(rel_sb, io["rel_bias"]).then_inc(table_in, 16)
            sp.dma_start(onehot, io["onehot"]).then_inc(table_in, 16)
            sp.dma_start(table, io["mask"]).then_inc(table_in, 16)
            load_piece(1)
            sp.dma_start(sinks[:, :], io["sinks"].to_broadcast([P, QA])).then_inc(sinks_in, 16)
            sp.dma_start(value_bias[:, 0:KVA * DH], io["b_in"][:, int(T_VA) * P:int(T_QB) * P]).then_inc(sinks_in, 16)
            sp.dma_start(value_bias[:, KVA * DH:], io["b_in"][:, int(T_VB) * P:int(T_GA) * P]).then_inc(sinks_in, 16)
            for p in range(2, N_PIECES - 1):
                load_piece(p)

            wg = io["w_gate"][0].rearrange("e (q c p) n -> e q p c n", c=2, p=P)
            wu = io["w_up"][0].rearrange("e (q c p) n -> e q p c n", c=2, p=P)
            wd = io["w_down"][0].rearrange("e (q c p) n -> e q p c n", c=2, p=P)

            def load(place, w, e, q, arrived):
                src = w[e, q] if isinstance(e, int) else w[bass.ds(e, 1), q].rearrange("o p c n -> (o p) c n")
                sp.dma_start(place[:, :, :], src).then_inc(arrived, 16)

            def load_gate_up(e, b, q):
                load(gate_w[b][q], wg, e, q, gate_in[b][q])
                load(up_w[b][q], wu, e, q, up_in[b][q])

            def load_expert(e, it, b):
                for q in range(QUADS):
                    sp.wait_ge(gu_used, (it - 2) * QUADS + q + 1)
                    load_gate_up(e, b, q)
                for q in range(QUADS):
                    sp.wait_ge(down_used, (it - 1) * QUADS + q + 1)
                    load(down_w[q], wd, e, q, down_in[q])

            def load_first(i):
                w, q = ((wg, wu)[i % 2], i // 2) if i < 2 * QUADS else (wd, i - 2 * QUADS)
                load(slot[i], w, 0, q, first_in[i])

            sp.wait_ge(mixT_up, 5)
            for i in range(3):
                load_first(i)
            load_piece(N_PIECES - 1)
            for i in range(RAW):
                sp.wait_ge(lo_done, N_PIECES - RAW + 1 + i)
                load_first(3 + i)
            sp.wait_ge(piece_up, W_OUT + 1)
            load_first(8)
            sp.wait_ge(piece_up, N_PIECES - 2)
            load_first(9)
            load_first(10)
            sp.wait_ge(piece_up, N_PIECES - 1)
            load_first(11)
            load(gate_w[1][0], wg, 1, 0, gate_in[1][0])
            sp.wait_ge(x2_up, TT)
            load(up_w[1][0], wu, 1, 0, up_in[1][0])
            for q in range(1, QUADS - 1):
                load_gate_up(1, 1, q)
            sp.wait_ge(logits_up, 1)
            load_gate_up(1, 1, QUADS - 1)
            for q in range(QUADS):
                sp.wait_ge(gu_used, 1 + q // 2)
                load(down_w[q], wd, 1, q, down_in[q])
            for q in range(QUADS):
                if q < 2:
                    sp.wait_ge(gu_used, 3 + q)
                else:
                    sp.wait_ge(down_used, 2 * (q - 1))
                load_gate_up(2, 0, q)
            for q in range(QUADS):
                sp.wait_ge(down_used, QUADS + q + 1)
                load(down_w[q], wd, 2, q, down_in[q])
            load_expert(3, 3, 1)
            with sp.Fori(2, E // 2) as t:
                for b in range(2):
                    load_expert(2 * t + b, 2 * t + b, b)
            sp.wait_ge(passes_done, 1)
            n = sp.value_load(further[0:1, 0:1], min_val=0, max_val=PASSES - 1)
            with sp.If(n > 0):
                with sp.Fori(1, n + 1) as p:
                    with sp.Fori(0, E // 2) as t:
                        for b in range(2):
                            load_expert(2 * t + b, p * E + 2 * t + b, b)
            for tt in range(TT):
                sp.wait_ge(result_done, tt + 1)
                sp.dma_start(out[0, tt * P:(tt + 1) * P, :], h2[:, tt, :]).then_inc(y_out, 16)
            sp.wait_ge(y_out, 16 * TT)

        @block.gpsimd
        def _(pool):
            pool.wait_ge(table_out, 16)
            for n, (_, heads) in enumerate(groups):
                if n >= 2:
                    pool.wait_ge(logits_done, first_unit[n - 1])
                src = bass.AP(scratch.tensor, heads[0] * 2 * S,
                              [[1, P], [(heads[1] - heads[0]) * 2 * S, len(heads)], [1, 3 * P]])
                pool.dma_start(windows[:, n % 2, 0:len(heads), :], src).then_inc(window_in[n % 2], 16)

        @block.scalar
        def _(act):
            roots = [0]

            def root(at, n):
                roots[0] += 1
                act.wait_ge(inverse_done, roots[0])
                nc.scalar.activation(stats[:, at:at + n], stats[:, at:at + n], ACT.Sqrt).then_inc(root_done, 1)

            def split_hi(p):
                if p >= N_PIECES:
                    return
                act.wait_ge(raw_in[p % RAW], 16 * (p // RAW + 1))
                if p >= SPLIT:
                    act.wait_ge(piece_up, p - SPLIT + 1)
                nc.scalar.copy(piece_hi[:, p % SPLIT, :], raw[:, p % RAW, :]).then_inc(hi_done, 1)

            def load_table(i, function):
                nc.scalar.activation(unused[:, i:i + 1], one[:, :], function)

            act.wait_ge(one_done, 1)
            load_table(0, ACT.Sqrt)
            for tt in range(TT):
                act.wait_ge(x_in[tt], 16)
                nc.scalar.activation(h[:, tt, :], x_sb[:, tt, :], ACT.Square,
                                     accum_out=stats[:, tt:tt + 1]).then_inc(sumsq_done, 1)
            for tt in range(TT):
                root(tt, 1)
            split_hi(0)
            act.wait_ge(columns_done, 1)
            for c in range(KC):
                if c % 2 == 0:
                    act.wait_ge(hT_up, c // 2 + 1)
                g = int(T_END) + c
                nc.scalar.activation(hT_hi[:, c, :], bank(2 + c // 2)[:, (c % 2) * S:(c % 2 + 1) * S], ACT.Copy,
                                     scale=columns[:, g:g + 1]).then_inc(hT_hi_done, 1)
            for p in range(1, SPLIT):
                split_hi(p)

            for p in range(GATE_A):
                if p == 1:
                    act.wait_ge(table_done, 1)
                    act.dma_start(scratch, table).then_inc(table_out, 16)
                act.wait_ge(piece_up, p + 1)
                src = bank(PROJ[p % 2]).rearrange("p (k s) -> p k s", k=2)
                if V_A <= p < Q_B or p >= V_B:
                    dst = va[:, :, :] if p < Q_B else vb[:, :, (p - V_B) * PIECE:(p - V_B + 1) * PIECE]
                    nc.scalar.copy(dst, src).then_inc(qkv_copied, 1)
                else:
                    for k in range(2):
                        t = 2 * p + k
                        if K_A <= p < V_A:
                            g = 2 * (t - int(T_KA))
                            for half in range(2):
                                r = slice(half * DH, (half + 1) * DH)
                                last = nc.scalar.activation(kaT[r, g + half, :], src[r, k, :], ACT.Identity,
                                                            bias=columns[r, t:t + 1])
                            continue
                        if p < K_A:
                            dst = qaT[:, t, ::-1]
                        elif p < K_B:
                            dst = qbT[:, t - int(T_QB), ::-1]
                        else:
                            dst = kbT[:, t - int(T_KB), :]
                        last = nc.scalar.activation(dst, src[:, k, :], ACT.Identity, bias=columns[:, t:t + 1])
                    last.then_inc(qkv_copied, 1)
                split_hi(p + SPLIT)

            def copy_turned(n):
                if n >= 2:
                    act.wait_ge(pv_up, n - 1)
                for i, u in enumerate(range(first_unit[n], first_unit[n + 1])):
                    act.wait_ge(turned_up, u + 1)
                    nc.scalar.copy(probsT[:, n % 2, i].rearrange("p a b c -> p (a b c)"),
                                   bank(TURN[u % 2])).then_inc(turned_copied, 1)

            def exps(n):
                kind, heads = groups[n]
                act.wait_ge(peaks_done, n + 1)
                if kind == "A":
                    for i in range(2):
                        for iq in range(2):
                            c = 2 * i + iq
                            v = probs[:, n % 3, i, iq, :]
                            nc.scalar.activation(v, v, ACT.Exp, bias=minus_peak[:, n % STATS, c:c + 1],
                                                 accum_out=den[:, n % STATS, c:c + 1]).then_inc(exps_done, 1)
                    act.wait_ge(sinks_sub, n - HB + 1)
                    v = sink_exp[:, n % STATS, :]
                    nc.scalar.activation(v, v, ACT.Exp).then_inc(sinks_done, 1)
                else:
                    for iq in range(2):
                        v = probs[:, n % 3, :, iq, :]
                        nc.scalar.activation(v, v, ACT.Exp, bias=minus_peak[:, n % STATS, iq:iq + 1],
                                             accum_out=den[:, n % STATS, iq:iq + 1]).then_inc(exps_done, 2)

            exps(0)
            for n in range(GROUPS):
                if n + 1 < GROUPS:
                    exps(n + 1)
                copy_turned(n)
                if n < N_GATE:
                    split_hi(GATE_A + n + SPLIT)
            def mix_hi(i):
                k = list(MIX)[i]
                act.wait_ge(mixT_up, i + 1)
                nc.scalar.copy(mixT_hi[:, 2 * k:2 * k + 2, ::-1],
                               bank(MIX[k]).rearrange("p (c s) -> p c s", c=2)).then_inc(mixT_hi_done, 1)

            def gate(i):
                v = gates[:, i].rearrange("p f s -> p (f s)")
                nc.scalar.activation(v, v, ACT.Sigmoid).then_inc(gates_done, 1)

            for i in range(3):
                mix_hi(i)
            act.wait_ge(pv_up, GROUPS)
            act.dma_start(gu_rows[:, 0, :], io["b_gate"][0]).then_inc(gu_rows_in, 16)
            act.dma_start(gu_rows[:, 1, :], io["b_up"][0]).then_inc(gu_rows_in, 16)
            act.dma_start(gain_ffn[:, :], io["norm_ffn"].to_broadcast([P, D])).then_inc(moe_in, 16)
            act.dma_start(router[:, :, :], io["router_w"][0].rearrange("(c p) e -> p c e", p=P)).then_inc(moe_in, 16)
            act.dma_start(router_row[:, :], io["router_b"]).then_inc(moe_in, 16)
            act.dma_start(down_bias[:, :], io["b_down"][0]).then_inc(moe_in, 16)
            mix_hi(3)
            act.wait_ge(gate_copied, N_GATE)
            gate(1)
            mix_hi(4)
            act.dma_start(x_sb[:, :, :], io["x"][0].rearrange("(t p) d -> p t d", p=P)).then_inc(x_again, 16)
            gate(0)
            act.wait_ge(gu_bias_up, 1)
            nc.scalar.copy(gu_bias[:, :, :, :].rearrange("p e c j -> p (c j) e"),
                           bank(GU_BIAS).rearrange("p (k e) -> p k e", e=E)).then_inc(gu_bias_done, 1)
            split_hi(W_B + SPLIT)
            for m in range(W_OUT - W_A):
                act.wait_ge(sum_done, m + 1)
                nc.scalar.copy(mergedT_hi[:, 2 * m:2 * m + 2, :].rearrange("p c s -> p (c s)"),
                               products[:, m % 2, :]).then_inc(merged_hi_done, 1)
                split_hi(W_A + m + SPLIT)
            split_hi(N_PIECES - 1)
            load_table(1, ACT.Sqrt)

            for tt in range(TT):
                act.wait_ge(x2_up, tt + 1)
                nc.scalar.activation(squares[:, tt, :], bank(Y + 2 * tt, 2), ACT.Square,
                                     accum_out=stats[:, 8 + tt:9 + tt]).then_inc(sumsq_done, 1)
                root(8 + tt, 1)
            act.dma_start(gain_final[:, :], io["norm_final"].unsqueeze(0).to_broadcast([P, D])).then_inc(gain_in, 16)
            for tt in range(TT):
                act.wait_ge(h2T_up, 2 * tt + 1)
                nc.scalar.copy(h2T[:, 0:KC // 2, tt * P:(tt + 1) * P],
                               bank(2 * tt).rearrange("p (c s) -> p c s", s=P)).then_inc(h2T_left, 1)
            for tt in range(TT):
                act.wait_ge(shift_done, 1)
                nc.scalar.activation(weights[:, tt, :], logits[:, tt, :], ACT.Exp,
                                     bias=few[:, tt:tt + 1]).then_inc(exp_done, 1)

            def copy_gathered(it):
                act.wait_ge(gather_up, it + 1)
                nc.scalar.copy(xT[:, :, :].rearrange("p c s -> p (c s)"), bank(GATHER)).then_inc(xT_done, 1)

            act.wait_ge(gather_half, 1)
            nc.scalar.copy(xT[:, 0:KC // 2, :].rearrange("p c s -> p (c s)"),
                           bank(GATHER)[:, 0:BANK // 2]).then_inc(xT_half, 1)
            act.wait_ge(gather_up, 1)
            nc.scalar.copy(xT[:, KC // 2:, :].rearrange("p c s -> p (c s)"),
                           bank(DOWN)[:, 0:BANK // 2]).then_inc(xT_done, 1)
            act.wait_ge(weightT_up, 1)
            nc.scalar.copy(weightT[:, :], bank(DOWN)[0:E, 0:S]).then_inc(weightT_done, 1)
            act.wait_ge(passes_done, 1)
            n_passes = act.value_load(further[0:1, 0:1], min_val=0, max_val=PASSES - 1) + 1
            load_table(2, ACT.Sigmoid)
            with act.Fori(0, n_passes) as p:
                with act.Fori(0, E) as e:
                    it = p * E + e
                    act.wait_ge(gu_half, it + 1)
                    nc.scalar.copy(gu[:, 0:BANK], bank(GU)).then_inc(gu_left, 1)
                    for half in range(2):
                        f = slice(half * KC // 2, (half + 1) * KC // 2)
                        act.wait_ge(gate_done, 2 * it + half + 1)
                        nc.scalar.activation(sig[:, f, :], gate_c[:, f, :], ACT.Sigmoid, scale=ALPHA).then_inc(sig_done, 1)
                    copy_gathered(it + 1)
                    act.wait_ge(down_used, it * QUADS + QUADS)
                    nc.scalar.copy(y_half[:, :], bank(DOWN)).then_inc(y_copied, 1)
            load_table(3, ACT.Sqrt)
            for tt in range(TT):
                act.wait_ge(y_up, tt + 1)
                nc.scalar.activation(h2[:, tt, :], bank(Y + 2 * tt, 2), ACT.Square,
                                     accum_out=stats[:, 16 + tt:17 + tt]).then_inc(sumsq_done, 1)
                root(16 + tt, 1)

        @block.tensor
        def _(pe):
            mm, tr = nc.tensor.matmul, nc.tensor.transpose

            def mm3(o, a_hi, a_lo, b_hi, b_lo, first, last, **more):
                mm(o, a_hi, b_hi, start=first, stop=False, **more)
                mm(o, a_hi, b_lo, start=False, stop=False, **more)
                return mm(o, a_lo, b_hi, start=False, stop=last, **more)

            pe.wait_ge(square_in, 16)
            pe.wait_ge(rows_in, 32)
            nr = int(T_END) + KC
            tr(bank(COLUMNS)[:, 0:nr], rows[:, :], ident[0:nr, 0:nr]).then_inc(columns_up, 1)
            for tt in range(TT):
                pe.wait_ge(h_done, tt + 1)
                for c in range(KC):
                    last = tr(bank(2 + c // 2)[:, (c % 2) * S + tt * P:(c % 2) * S + (tt + 1) * P],
                              h[:, tt, c * P:(c + 1) * P], ident)
                    if tt == TT - 1 and c % 2:
                        last.then_inc(hT_up, 1)

            def project(p):
                if p > 0:
                    pe.wait_ge(lo_done, p + 1)
                if p >= 2:
                    pe.wait_ge(qkv_copied, min(p - 1, GATE_A))
                if p - 1 > GATE_A:
                    pe.wait_ge(gate_copied, p - 1 - GATE_A)
                hi = piece_hi[:, p % SPLIT, :].rearrange("p (c n) -> p c n", c=KC)
                lo = piece_lo[:, p % SPLIT, :].rearrange("p (c n) -> p c n", c=KC)
                values = V_A <= p < Q_B or V_B <= p < GATE_A
                for k in range(2):
                    o = bank(PROJ[p % 2])[:, k * S:(k + 1) * S]
                    r = slice(k * P, (k + 1) * P)
                    if p == 0 and k == 0:
                        pe.wait_ge(hi_done, 1)
                        for c in range(KC):
                            pe.wait_ge(hT_hi_done, c + 1)
                            mm(o, hi[:, c, r], hT_hi[:, c, :], start=c == 0, stop=False)
                        pe.wait_ge(lo_done, 1)
                        for c in range(KC):
                            mm(o, lo[:, c, r], hT_hi[:, c, :], start=False, stop=False)
                        for c in range(KC):
                            pe.wait_ge(hT_lo_done, c + 1)
                            mm(o, hi[:, c, r], hT_lo[:, c, :], start=False, stop=c == KC - 1)
                        continue
                    for c in range(KC):
                        if values:
                            last = mm3(o, hT_hi[:, c, r], hT_lo[:, c, r], hi[:, c, :], lo[:, c, :], c == 0, False)
                        else:
                            last = mm3(o, hi[:, c, r], lo[:, c, r], hT_hi[:, c, :], hT_lo[:, c, :], c == 0, c == KC - 1)
                    if values:
                        pe.wait_ge(sinks_in, 48)
                        r0 = 0 if p < Q_B else (1 + p - V_B) * PIECE
                        last = mm(o, ones[0:1, :], value_bias[0:1, r0:r0 + PIECE], start=False, stop=True)
                last.then_inc(piece_up, 1)


            def scores(n, some):
                kind, heads = groups[n]
                if n == HB:
                    pe.wait_ge(keys_done, 1)
                for i, head in list(enumerate(heads))[some]:
                    u = first_unit[n] + i
                    if u >= 2:
                        pe.wait_ge(logits_done, u - 1)
                    if kind == "A":
                        r = slice((head % 2) * DH, (head % 2 + 1) * DH)
                        q, k = qaT[r, head // 2, :], kaT[r, head // (QA // KVA), :]
                    else:
                        hb = n
                        r = slice((hb % 2) * DH, (hb % 2 + 1) * DH)
                        q, k = qbT[r, 2 * i + hb // 2, :], kbT[r, 2 * i + hb // 2, :]
                    for iq in range(2):
                        last = mm(bank(SCORE[u % 2])[:, iq * S:(iq + 1) * S], q[:, iq * P:(iq + 1) * P], k,
                                  start=True, stop=True)
                    last.then_inc(scores_up, 1)

            def turn(n):
                pe.wait_ge(exps_done, 4 * (n + 1))
                for i in range(len(groups[n][1])):
                    u = first_unit[n] + i
                    if u >= 2:
                        pe.wait_ge(turned_copied, u - 1)
                    for jt in range(TT):
                        for iq in range(2):
                            at = (jt * 2 + iq) * P
                            last = tr(bank(TURN[u % 2])[:, at:at + P], probs[:, n % 3, i, iq, jt * P:(jt + 1) * P], ident)
                    last.then_inc(turned_up, 1)

            def weigh(n):
                kind, heads = groups[n]
                pe.wait_ge(turned_copied, first_unit[n + 1])
                if n >= 2:
                    pe.wait_ge(mix_done, n - 1)
                for iq in range(2):
                    if kind == "A":
                        for i, head in enumerate(heads):
                            o = bank(PV[n % 2])[:, (iq * 2 + i) * DH:(iq * 2 + i + 1) * DH]
                            kv = head // (QA // KVA)
                            for jt in range(TT):
                                last = mm(o, probsT[:, n % 2, i, jt, iq, :], va[:, jt, kv * DH:(kv + 1) * DH],
                                          start=jt == 0, stop=jt == TT - 1)
                    else:
                        o = bank(PV[n % 2])[:, iq * 2 * DH:iq * 2 * DH + DH]
                        for g in range(NG):
                            col = (g * HB + n) * DH
                            for jt in range(TT):
                                last = mm(o, probsT[:, n % 2, g, jt, iq, :], vb[:, jt, col:col + DH],
                                          start=g == 0 and jt == 0, stop=g == NG - 1 and jt == TT - 1)
                last.then_inc(pv_up, 1)

            def turn_mix(k):
                for c in (2 * k, 2 * k + 1):
                    for tt in range(TT):
                        src = x_sb[:, tt, c * P:(c + 1) * P] if c < KC else yb[:, tt, (c - KC) * P:(c - KC + 1) * P]
                        last = tr(bank(MIX[k])[:, (c % 2) * S + tt * P:(c % 2) * S + (tt + 1) * P], src, ident)
                last.then_inc(mixT_up, 1)

            FIRST, REST = slice(0, 2), slice(2, None)
            project(0)
            pe.wait_ge(table_in, 48)
            mm(bank(TABLE)[0:NU, :], rel_sb, onehot, start=True, stop=True).then_inc(table_up, 1)
            for p in range(1, V_B):
                project(p)
            pe.wait_ge(qkv_copied, V_B)
            scores(0, FIRST)
            project(V_B)
            scores(0, REST)
            scores(1, slice(0, 1))
            project(V_B + 1)
            scores(1, slice(1, None))
            for p in range(V_B + 2, GATE_A):
                project(p)
            for n in range(GROUPS):
                if n + 2 < GROUPS:
                    scores(n + 2, FIRST)
                if n < N_GATE:
                    project(GATE_A + n)
                if n + 2 < GROUPS:
                    scores(n + 2, REST)
                turn(n)
                if n >= 1:
                    weigh(n - 1)
            pe.wait_ge(logits_done, first_unit[GROUPS])
            pe.wait_ge(gate_copied, N_GATE)
            pe.wait_ge(mix_done, HB + 4)
            for k in (4, 0, 1):
                turn_mix(k)
            weigh(GROUPS - 1)
            pe.wait_ge(mix_done, HB + 6)
            turn_mix(2)

            def parts(p, c):
                pe.wait_ge(lo_done, p + 1)
                return (piece_hi[:, p % SPLIT, :].rearrange("p (c n) -> p c n", c=c),
                        piece_lo[:, p % SPLIT, :].rearrange("p (c n) -> p c n", c=c))

            hi, lo = parts(W_B, 2)
            pe.wait_ge(mixT_lo_done, 1)
            for f in range(KC):
                if f == KC // 2:
                    pe.wait_ge(mix_done, GROUPS)
                    turn_mix(3)
                    pe.wait_ge(gu_rows_in, 32)
                    pe.wait_ge(mixT_lo_done, 2)
                    for c in range(KC):
                        for j in range(2):
                            at = (c * 2 + j) * E
                            last = tr(bank(GU_BIAS)[:, at:at + E], gu_rows[:, j, c * P:(c + 1) * P], ident[0:E, 0:E])
                    last.then_inc(gu_bias_up, 1)
                for c in range(2):
                    o = psum[:, WIDE * BANK + f * S:WIDE * BANK + (f + 1) * S]
                    r = slice(f * P, (f + 1) * P)
                    last = mm3(o, hi[:, c, r], lo[:, c, r], mixT_hi[:, KC + c, :], mixT_lo[:, KC + c, :], c == 0, c == 1)
            last.then_inc(piece_up, 1)
            pe.wait_ge(mixT_lo_done, 5)
            for m in range(W_OUT - W_A):
                hi, lo = parts(W_A + m, KC)
                if m >= 2:
                    pe.wait_ge(products_done, m - 1)
                for k in range(2):
                    r = slice(k * P, (k + 1) * P)
                    for c in range(KC):
                        last = mm3(bank(PROJ[m % 2])[:, k * S:(k + 1) * S], hi[:, c, r], lo[:, c, r],
                                   mixT_hi[:, c, :], mixT_lo[:, c, :], c == 0, c == KC - 1)
                last.then_inc(piece_up, 1)
            pe.wait_ge(branch_b_done, 4)
            pe.wait_ge(x_again, 16)
            for tt in range(TT):
                for nb in range(2):
                    mm(bank(Y + 2 * tt + nb), ident, x_sb[:, tt, nb * BANK:(nb + 1) * BANK], start=True, stop=False,
                       skip_group_check=True)
            for m in range(N_PIECES - W_OUT):
                hi, lo = parts(W_OUT + m, 2)
                pe.wait_ge(merged_lo_done, m + 1)
                for tt in range(TT):
                    for k in range(2):
                        c = 2 * m + k
                        r = slice(tt * P, (tt + 1) * P)
                        for nb in range(2):
                            cols = slice(nb * BANK, (nb + 1) * BANK)
                            last = mm3(bank(Y + 2 * tt + nb), mergedT_hi[:, c, r], mergedT_lo[:, c, r],
                                       hi[:, k, cols], lo[:, k, cols], False, False, skip_group_check=True)
                    if W_OUT + m == N_PIECES - 1:
                        last.then_inc(x2_up, 1)
                if W_OUT + m < N_PIECES - 1:
                    last.then_inc(piece_up, 1)

            def keep_clock(to, n):
                for _ in range(n):
                    mm(bank(to), ident, h2[:, 0, 0:BANK], start=True, stop=True)

            for tt in range(TT):
                if tt == 1:
                    keep_clock(3, 2)
                for c in range(KC):
                    if c % 4 == 0:
                        pe.wait_ge(h2_done, 2 * tt + c // 4 + 1)
                    last = tr(bank(2 * tt + c // 4)[:, (c % 4) * P:(c % 4 + 1) * P], h2[:, tt, c * P:(c + 1) * P], ident)
                    if c % 4 == 3:
                        last.then_inc(h2T_up, 1)
            pe.wait_ge(moe_in, 64)
            for tt in range(TT):
                o = bank(LOGITS)[:, tt * E:(tt + 1) * E]
                pe.wait_ge(h2T_left, tt + 1)
                for c in range(KC):
                    if c == KC // 2:
                        pe.wait_ge(h2T_right, tt + 1)
                    mm(o, h2T[:, c, tt * P:(tt + 1) * P], router[:, c, :], start=c == 0, stop=False)
                last = mm(o, ones[0:1, :], router_row[0:1, :], start=False, stop=True)
            last.then_inc(logits_up, 1)
            keep_clock(GATHER, 4)
            pe.wait_ge(chosen_done, 1)
            mm(bank(RANKS)[:, 0:E], tri, chosen[:, 0, :], start=True, stop=True)
            mm(bank(RANKS)[:, E:2 * E], ones, chosen[:, 0, :], start=True, stop=False)
            mm(bank(RANKS)[:, E:2 * E], tri, chosen[:, 1, :], start=False, stop=True)
            mm(bank(RANKS)[:, 2 * E:3 * E], ones, chosen[:, 0, :], start=True, stop=False)
            mm(bank(RANKS)[:, 2 * E:3 * E], ones, chosen[:, 1, :], start=False, stop=True).then_inc(rank_up, 1)

            def gather(it, halves=False):
                pe.wait_ge(pick_done, it + 1)
                for c in range(KC):
                    o = bank(GATHER)[:, c * CAP:(c + 1) * CAP]
                    if halves and c >= KC // 2:
                        o = bank(DOWN)[:, (c - KC // 2) * CAP:(c - KC // 2 + 1) * CAP]
                    for tt in range(TT):
                        last = mm(o, h2[:, tt, c * P:(c + 1) * P], pick[:, tt, :], start=tt == 0, stop=tt == TT - 1)
                    if halves and c == KC // 2 - 1:
                        last.then_inc(gather_half, 1)
                last.then_inc(gather_up, 1)

            def turn_spread(it):
                pe.wait_ge(spread_done, it + 1)
                pe.wait_ge(xT_done, it + 2)
                for tt in range(TT):
                    last = tr(bank(GATHER)[:, tt * P:(tt + 1) * P], spread[:, tt, :], ident)
                last.then_inc(spreadT_up, 1)

            def add_to_tokens(tt):
                for half in range(2):
                    r = slice(half * CAP, (half + 1) * CAP)
                    last = mm(bank(Y + 2 * tt + half), spreadT[r, tt * P:(tt + 1) * P], y_half[r, :],
                              start=False, stop=False, skip_group_check=True)
                return last

            def turn_gate_up(it, half):
                pe.wait_ge((gu_left, gu_right)[half], it + 1)
                for c in range(half * KC // 2, (half + 1) * KC // 2):
                    last = tr(bank(GU + half)[:, (c % 4) * P:(c % 4 + 1) * P], gu[:, c * P:(c + 1) * P], ident)
                last.then_inc(guT_up, 1)

            def step(it, turn, b, first=False, final=False):
                if first:
                    pe.wait_ge(xT_half, 1)
                else:
                    pe.wait_ge(xT_done, it + 1)
                for q in range(QUADS):
                    if final and q == 1:
                        pe.wait_ge(weightT_done, 1)
                        for tt in range(TT):
                            for nb in range(2):
                                mm(bank(Y + 2 * tt + nb), weightT[:, tt * P:(tt + 1) * P],
                                   down_bias[:, nb * BANK:(nb + 1) * BANK], start=False, stop=False,
                                   skip_group_check=True)
                    if final and q == 2:
                        pe.wait_ge(y_copied, it)
                        pe.wait_ge(spreadT_done, it)
                        for tt in range(TT):
                            add_to_tokens(tt)
                        pe.wait_ge(pick_done, it + 2)
                        mm(bank(GATHER)[:, 0:CAP], h2[:, 0, 0:P], pick[:, 0, :], start=True,
                           stop=True).then_inc(gather_up, 1)
                    if first:
                        gate, up = slot[2 * q], slot[2 * q + 1]
                        pe.wait_ge(first_in[2 * q], 16)
                        pe.wait_ge(first_in[2 * q + 1], 16)
                    else:
                        gate, up = gate_w[b][q], up_w[b][q]
                        pe.wait_ge(gate_in[b][q], 16 * turn)
                        pe.wait_ge(up_in[b][q], 16 * turn)
                    if first and q == QUADS // 2:
                        pe.wait_ge(xT_done, 1)
                        pe.wait_ge(weight_done, 1)
                        for tt in range(TT):
                            last = tr(bank(DOWN)[0:E, tt * P:(tt + 1) * P], weights[:, tt, :], ident)
                        last.then_inc(weightT_up, 1)
                    for nb, c in [(0, 0), (0, 1), (1, 0), (1, 1)]:
                        k = 2 * q + c
                        cols = slice(nb * BANK, (nb + 1) * BANK)
                        mm(bank(GU + nb)[0:CAP, :], xT[:, k, :], gate[:, c, cols],
                           start=k == 0, stop=k == KC - 1)
                        last = mm(bank(GU + nb)[CAP:P, :], xT[:, k, :], up[:, c, cols],
                                  start=k == 0, stop=k == KC - 1)
                        if q == QUADS - 1 and (nb, c) == (0, 1):
                            last.then_inc(gu_half, 1)
                    last.then_inc(gu_used, 1)
                turn_gate_up(it, 0)
                if not first and not final:
                    pe.wait_ge(y_copied, it)
                    pe.wait_ge(spreadT_done, it)
                    add_to_tokens(0)
                turn_gate_up(it, 1)
                if not first and not final:
                    add_to_tokens(1)
                if not final:
                    gather(it + 1)
                for q in range(QUADS):
                    down = slot[2 * QUADS + q] if first else down_w[q]
                    if q % 2 == 0:
                        pe.wait_ge(hidden_done, 2 * it + q // 2 + 1)
                    if first:
                        pe.wait_ge(first_in[2 * QUADS + q], 16)
                    else:
                        pe.wait_ge(down_in[q], 16 * it)
                    if q == QUADS - 1:
                        turn_spread(it)
                    for c in range(2):
                        k = 2 * q + c
                        for half in range(2):
                            last = mm(bank(DOWN)[half * CAP:(half + 1) * CAP, :], hidden[:, k, :],
                                      down[:, c, half * BANK:(half + 1) * BANK], start=k == 0, stop=k == KC - 1)
                    last.then_inc(down_used, 1)

            gather(0, halves=True)
            pe.wait_ge(passes_done, 1)
            n = pe.value_load(further[0:1, 0:1], min_val=0, max_val=PASSES - 1)
            n_pairs, last_step = n * (E // 2) + E // 2, n * E + (E - 1)
            step(0, 0, 0, first=True)
            with pe.Fori(1, n_pairs) as t:
                step(2 * t - 1, t, 1)
                step(2 * t, t, 0)
            step(last_step, n_pairs, 1, final=True)
            pe.wait_ge(y_copied, last_step + 1)
            pe.wait_ge(spreadT_done, last_step + 1)
            for tt in range(TT):
                add_to_tokens(tt).then_inc(y_up, 1)

        @block.vector
        def _(dve):
            v = nc.vector
            done, roots = [0], [0]

            def step(ins):
                done[0] += 1
                ins.then_inc(vec, 1)
                dve.wait_ge(vec, done[0])

            def inverse_rms(at, n, n_sumsq):
                dve.wait_ge(sumsq_done, n_sumsq)
                r = stats[:, at:at + n]
                step(v.tensor_scalar(r, r, 1.0 / D, EPS, ALU.mult, ALU.add))
                v.reciprocal(r, r).then_inc(inverse_done, 1)
                roots[0] += 1
                dve.wait_ge(root_done, roots[0])

            def split_lo(p):
                if p >= N_PIECES:
                    return
                dve.wait_ge(hi_done, p + 1)
                v.tensor_tensor(piece_lo[:, p % SPLIT, :], raw[:, p % RAW, :],
                                piece_hi[:, p % SPLIT, :].bitcast(F32), ALU.subtract).then_inc(lo_done, 1)

            v.memset(one[:, :], 1.0).then_inc(one_done, 1)
            for tt in range(TT):
                if tt == 1:
                    dve.wait_ge(columns_up, 1)
                    v.tensor_copy(columns[:, :], bank(COLUMNS)[:, 0:int(T_END) + KC]).then_inc(columns_done, 1)
                inverse_rms(tt, 1, tt + 1)
                v.tensor_scalar(h[:, tt, :], x_sb[:, tt, :], stats[:, tt:tt + 1], None, ALU.mult).then_inc(h_done, 1)
            split_lo(0)
            for c in range(KC):
                dve.wait_ge(hT_hi_done, 2 * (c // 2) + 2)
                g = int(T_END) + c
                v.scalar_tensor_tensor(hT_lo[:, c, :], bank(2 + c // 2)[:, (c % 2) * S:(c % 2 + 1) * S],
                                       columns[:, g:g + 1], hT_hi[:, c, :].bitcast(F32), ALU.mult,
                                       ALU.subtract).then_inc(hT_lo_done, 1)
            def copy_gates(p):
                dve.wait_ge(piece_up, p + 1)
                for k in range(2):
                    t = 2 * p + k
                    f = t - int(T_GA)
                    last = v.tensor_scalar(gates[:, f // KC, f % KC, :], bank(PROJ[p % 2])[:, k * S:(k + 1) * S],
                                           columns[:, t:t + 1], None, ALU.add)
                last.then_inc(gate_copied, 1)

            def logits_of(n, some):
                kind, heads = groups[n]
                if n >= 3:
                    dve.wait_ge(turned_up, first_unit[n - 2])
                dve.wait_ge(window_in[n % 2], 16 * (n // 2 + 1))
                for i in range(len(heads))[some]:
                    u = first_unit[n] + i
                    dve.wait_ge(scores_up, u + 1)
                    last = v.scalar_tensor_tensor(probs[:, n % 3, i, :, :], bank(SCORE[u % 2]).rearrange(
                        "p (a b) -> p a b", a=2), SCALE, window(n, i), ALU.mult, ALU.add)
                    last.then_inc(logits_done, 1)

            def peaks(n):
                kind, heads = groups[n]
                dve.wait_ge(logits_done, first_unit[n + 1])
                w = n % STATS
                if kind == "A":
                    step(v.tensor_reduce(peak[:, w, :], probs[:, n % 3, 0:2, :, :].rearrange(
                        "p i q s -> p (i q) s"), AX.X, ALU.max))
                    sk = sinks[:, heads[0]:heads[0] + 2].unsqueeze(2).to_broadcast([P, 2, 2])
                    pk = peak[:, w, :].rearrange("p (i q) -> p i q", i=2)
                    step(v.tensor_tensor(pk, pk, sk, ALU.max))
                    v.tensor_scalar(minus_peak[:, w, :], peak[:, w, :], -1.0, None, ALU.mult).then_inc(peaks_done, 1)
                    v.tensor_tensor(sink_exp[:, w, :].rearrange("p (i q) -> p i q", i=2), sk, pk,
                                    ALU.subtract).then_inc(sinks_sub, 1)
                else:
                    step(v.tensor_reduce(peak[:, w, 0:2], probs[:, n % 3, :, :, :].rearrange(
                        "p i q s -> p q i s"), AX.XY, ALU.max))
                    v.tensor_scalar(minus_peak[:, w, 0:2], peak[:, w, 0:2], -1.0, None, ALU.mult).then_inc(peaks_done, 1)

            def divide(n):
                kind, heads = groups[n]
                d = den[:, n % STATS, :]
                dve.wait_ge(exps_done, 4 * (n + 1))
                if kind == "A":
                    dve.wait_ge(sinks_done, n - HB + 1)
                    step(v.tensor_tensor(d, d, sink_exp[:, n % STATS, :], ALU.add))
                    step(v.reciprocal(d, d))
                else:
                    step(v.reciprocal(d[:, 0:2], d[:, 0:2]))
                dve.wait_ge(pv_up, n + 1)
                for iq in range(2):
                    if kind == "A":
                        last = v.tensor_tensor(
                            x_sb[:, iq, heads[0] * DH:(heads[0] + 2) * DH].rearrange("p (i d) -> p i d", i=2),
                            bank(PV[n % 2])[:, iq * 2 * DH:(iq + 1) * 2 * DH].rearrange("p (i d) -> p i d", i=2),
                            d.rearrange("p (i q) -> p i q", i=2)[:, :, iq:iq + 1].to_broadcast([P, 2, DH]), ALU.mult)
                    else:
                        col = n * DH
                        last = v.tensor_scalar(yb[:, iq, col:col + DH], bank(PV[n % 2])[:, iq * 2 * DH:iq * 2 * DH + DH],
                                               d[:, iq:iq + 1], None, ALU.mult)
                last.then_inc(mix_done, 1)

            for p in range(1, SPLIT):
                split_lo(p)
            dve.wait_ge(table_up, 1)
            v.tensor_tensor(table, table, bank(TABLE)[0:NU, :], ALU.add).then_inc(table_done, 1)
            for p in range(GATE_A):
                split_lo(p + SPLIT)
                if p == V_A:
                    dve.wait_ge(qkv_copied, V_A)
                    v.tensor_copy(kaT[DH:P, 0::2, :], kaT[0:DH, 0::2, :])
                    v.tensor_copy(kaT[0:DH, 1::2, :], kaT[DH:P, 1::2, :]).then_inc(keys_done, 1)
                if p == V_B - 1:
                    logits_of(0, slice(0, 2))
                if p == V_B:
                    logits_of(0, slice(2, None))
                    peaks(0)
                    logits_of(1, slice(0, 1))
                if p == V_B + 1:
                    logits_of(1, slice(1, None))
                    peaks(1)
            for n in range(GROUPS):
                if n + 2 < GROUPS:
                    logits_of(n + 2, slice(None))
                    peaks(n + 2)
                if n < N_GATE:
                    copy_gates(GATE_A + n)
                    split_lo(GATE_A + n + SPLIT)
                if n >= 2:
                    divide(n - 2)
            divide(GROUPS - 2)
            divide(GROUPS - 1)

            for i, k in enumerate(MIX):
                dve.wait_ge(mixT_hi_done, i + 1)
                v.tensor_tensor(mixT_lo[:, 2 * k:2 * k + 2, ::-1], bank(MIX[k]).rearrange("p (c s) -> p c s", c=2),
                                mixT_hi[:, 2 * k:2 * k + 2, ::-1].bitcast(F32), ALU.subtract).then_inc(mixT_lo_done, 1)
            dve.wait_ge(gates_done, 1)
            dve.wait_ge(piece_up, W_B + 1)
            for k in range(4):
                g = gates[:, 1, 2 * k:2 * k + 2, :].rearrange("p f s -> p (f s)")
                v.tensor_tensor(g, g, bank(WIDE + k), ALU.mult).then_inc(branch_b_done, 1)
            split_lo(W_B + SPLIT)
            dve.wait_ge(gates_done, 2)
            for m in range(W_OUT - W_A):
                dve.wait_ge(piece_up, W_A + m + 1)
                if m >= 2:
                    dve.wait_ge(merged_hi_done, m - 1)
                g = gates[:, :, 2 * m:2 * m + 2, :].rearrange("p j f s -> p j (f s)")
                v.tensor_tensor(products[:, m % 2, :], g[:, 0, :], bank(PROJ[m % 2]), ALU.mult).then_inc(products_done, 1)
                dve.wait_ge(products_done, m + 1)
                dve.wait_ge(branch_b_done, 4)
                v.tensor_tensor(products[:, m % 2, :], products[:, m % 2, :], g[:, 1, :], ALU.add).then_inc(sum_done, 1)
                dve.wait_ge(sum_done, m + 1)
                dve.wait_ge(merged_hi_done, m + 1)
                v.tensor_tensor(mergedT_lo[:, 2 * m:2 * m + 2, :].rearrange("p c s -> p (c s)"), products[:, m % 2, :],
                                mergedT_hi[:, 2 * m:2 * m + 2, :].bitcast(F32).rearrange("p c s -> p (c s)"),
                                ALU.subtract).then_inc(merged_lo_done, 1)
                split_lo(W_A + m + SPLIT)
            split_lo(N_PIECES - 1)
            v.memset(rank[:, :, :], FAR)
            dve.wait_ge(moe_in, 64)
            for tt in range(TT):
                inverse_rms(8 + tt, 1, TT + tt + 1)
                for nb in range(2):
                    cols = slice(nb * BANK, (nb + 1) * BANK)
                    v.scalar_tensor_tensor(h2[:, tt, cols], bank(Y + 2 * tt + nb), stats[:, 8 + tt:9 + tt],
                                           gain_ffn[:, cols], ALU.mult, ALU.mult).then_inc(h2_done, 1)
            for tt in range(TT):
                dve.wait_ge(h2T_up, 2 * tt + 2)
                v.tensor_copy(h2T[:, KC // 2:, tt * P:(tt + 1) * P],
                              bank(2 * tt + 1).rearrange("p (c s) -> p c s", s=P)).then_inc(h2T_right, 1)

            dve.wait_ge(logits_up, 1)
            step(v.tensor_copy(logits[:, :, :], bank(LOGITS)[:, 0:TT * E].rearrange("p (t e) -> p t e", t=TT)))
            for tt in range(TT):
                step(v.max(top8[:, tt, :], logits[:, tt, :]))
            fourth = top8[:, :, TOPK - 1:TOPK].to_broadcast([P, TT, E])
            v.tensor_tensor(chosen[:, :, :], logits[:, :, :], fourth, ALU.is_gt)
            step(v.tensor_tensor(at_edge[:, :, :], logits[:, :, :], fourth, ALU.is_equal))
            step(v.tensor_reduce(few[:, 2:2 + TT], chosen[:, :, :], AX.X, ALU.add))
            step(v.tensor_scalar(few[:, 2:2 + TT], few[:, 2:2 + TT], -1.0, float(TOPK), ALU.mult, ALU.add))
            for tt in range(TT):
                step(v.tensor_tensor_scan(running[:, tt, :], ones[:, 0:E], at_edge[:, tt, :], 0.0, ALU.mult, ALU.add))
                step(v.tensor_scalar(running[:, tt, :], running[:, tt, :], few[:, 2 + tt:3 + tt], None, ALU.is_le))
            step(v.tensor_tensor(at_edge[:, :, :], at_edge[:, :, :], running[:, :, :], ALU.mult))
            v.tensor_tensor(chosen[:, :, :], chosen[:, :, :], at_edge[:, :, :], ALU.add).then_inc(chosen_done, 1)
            v.tensor_scalar(few[:, 0:TT], top8[:, :, 0], -1.0, None, ALU.mult).then_inc(shift_done, 1)
            dve.wait_ge(chosen_done, 1)
            step(v.tensor_scalar(running[:, :, :], chosen[:, :, :], -FAR, FAR, ALU.mult, ALU.add))
            dve.wait_ge(rank_up, 1)
            step(v.tensor_tensor(rank[:, :, 0:E], running[:, :, :],
                                 bank(RANKS)[:, 0:TT * E].rearrange("p (t e) -> p t e", t=TT), ALU.add))

            def build_pick(it):
                for tt in range(TT):
                    last = v.tensor_scalar(pick[:, tt, :], slots[:, 0:CAP], rank[:, tt, bass.ds(it, 1)], None,
                                           ALU.is_equal)
                last.then_inc(pick_done, 1)

            def build_spread(it, e):
                for tt in range(TT):
                    last = v.tensor_scalar(spread[:, tt, :], slots, rank[:, tt, bass.ds(it, 1)],
                                           weights[:, tt, bass.ds(e, 1)], ALU.is_equal, ALU.mult)
                last.then_inc(spread_done, 1)

            build_pick(0)
            for p in range(1, PASSES):
                step(v.tensor_scalar(rank[:, :, p * E:(p + 1) * E], rank[:, :, 0:E], float(-CAP * p), None, ALU.add))
            dve.wait_ge(exp_done, TT)
            step(v.tensor_tensor(weights[:, :, :], weights[:, :, :], chosen[:, :, :], ALU.mult))
            step(v.tensor_reduce(few[:, 4:4 + TT], weights[:, :, :], AX.X, ALU.add))
            step(v.reciprocal(few[:, 4:4 + TT], few[:, 4:4 + TT]))
            v.tensor_tensor(weights[:, :, :], weights[:, :, :], few[:, 4:4 + TT].unsqueeze(2).to_broadcast([P, TT, E]),
                            ALU.mult).then_inc(weight_done, 1)
            dve.wait_ge(weight_done, 1)
            step(v.tensor_reduce(few[0:1, 8:9], bank(RANKS)[0:1, 2 * E:3 * E], AX.X, ALU.max))
            for p in range(1, PASSES):
                step(v.tensor_scalar(few[0:1, 8 + p:9 + p], few[0:1, 8:9], float(CAP * p), None, ALU.is_gt))
            step(v.tensor_reduce(few[0:1, 12:13], few[0:1, 9:8 + PASSES], AX.X, ALU.add))
            v.tensor_copy(further[:, :], few[0:1, 12:13]).then_inc(passes_done, 1)

            dve.wait_ge(passes_done, 1)
            n_passes = dve.value_load(further[0:1, 0:1], min_val=0, max_val=PASSES - 1) + 1
            with dve.Fori(0, n_passes) as p:
                with dve.Fori(0, E) as e:
                    it = p * E + e
                    dve.wait_ge(gather_up, it + 1)
                    build_pick(it + 1)
                    dve.wait_ge(gu_used, it * QUADS + QUADS)
                    v.tensor_copy(gu[:, BANK:D], bank(GU + 1)).then_inc(gu_right, 1)
                    for half in range(2):
                        f = slice(half * KC // 2, (half + 1) * KC // 2)
                        n = 2 * it + half + 1
                        dve.wait_ge(guT_up, n)
                        v.tensor_tensor(guT[:, f, :, :].rearrange("p c j s -> p (c j) s"),
                                        bank(GU + half).rearrange("p (k s) -> p k s", s=CAP),
                                        gu_bias[:, bass.ds(e, 1), f, :].rearrange("p o c j -> p (o c j)").unsqueeze(2)
                                        .to_broadcast([P, KC, CAP]), ALU.add).then_inc(guT_done, 1)
                        dve.wait_ge(guT_done, n)
                        v.tensor_scalar(gate_c[:, f, :], guT[:, f, 0, :], LIMIT, None, ALU.min).then_inc(gate_done, 1)
                        v.tensor_scalar(up_c[:, f, :], guT[:, f, 1, :], -LIMIT, LIMIT, ALU.max,
                                        ALU.min).then_inc(up_done, 1)
                        dve.wait_ge(up_done, n)
                        dve.wait_ge(gate_done, n)
                        v.scalar_tensor_tensor(up_c[:, f, :], up_c[:, f, :], 1.0, gate_c[:, f, :], ALU.add,
                                               ALU.mult).then_inc(gated_done, 1)
                        dve.wait_ge(gated_done, n)
                        dve.wait_ge(sig_done, n)
                        v.tensor_tensor(hidden[:, f, :], up_c[:, f, :], sig[:, f, :], ALU.mult).then_inc(hidden_done, 1)
                    build_spread(it, e)
                    dve.wait_ge(spreadT_up, it + 1)
                    v.tensor_copy(spreadT[:, :], bank(GATHER)[:, 0:S]).then_inc(spreadT_done, 1)

            dve.wait_ge(gain_in, 16)
            for tt in range(TT):
                inverse_rms(16 + tt, 1, 2 * TT + tt + 1)
                v.scalar_tensor_tensor(h2[:, tt, :], bank(Y + 2 * tt, 2), stats[:, 16 + tt:17 + tt], gain_final[:, :],
                                       ALU.mult, ALU.mult).then_inc(result_done, 1)


INPUTS = ["x", "norm_mix", "w_in", "b_in", "sinks", "rel_bias", "w_branch_a", "w_branch_b", "w_out", "norm_ffn",
          "router_w", "router_b", "w_gate", "b_gate", "w_up", "b_up", "w_down", "b_down", "norm_final"]


def kernel(**inputs):
    import concourse.bacc as bacc
    from concourse.bass_utils import run_bass_kernel_spmd

    nc = bacc.Bacc("TRN2", target_bir_lowering=False, num_devices=1)
    given = {name: np.ascontiguousarray(inputs[name]) for name in INPUTS}
    given.update(constants())
    arrays, io = {}, {}
    for name, a in given.items():
        arrays[f"in_{name}"] = a
        io[name] = nc.dram_tensor(f"in_{name}", a.shape, mybir.dt.from_np(a.dtype), kind="ExternalInput").ap()
    out = nc.dram_tensor("out", (1, S, D), F32, kind="ExternalOutput").ap()
    scratch = nc.dram_tensor("bias_table", (NU, 2 * S), F32, kind="Internal").ap()
    build(nc, io, out, scratch)
    r = run_bass_kernel_spmd(nc, [arrays], core_ids=[0])
    return r.results[0]["out"]
```
